# Optimizing a Trainium2 kernel written in Bass

```python
import jax, jax.numpy as jnp
from jax import lax
import numpy as np

D_MODEL = 1024
BATCH = 1
SEQ = 512
DEPTH = 2

EPS = 1e-6
ROPE_BASE = 10000.0
MASK_VALUE = -1e30
LOG_FLOOR = 1e-20

HG_HEADS = 4
HG_DK = 128
HG_DV = 128
HG_WIDTH = HG_HEADS * HG_DV
HG_CHUNK = 64

MLA_HEADS = 8
MLA_D_NOPE = 64
MLA_D_ROPE = 32
MLA_D_V = 64
MLA_D_C = 256
MLA_D_CQ = 768
MLA_WIDTH = MLA_HEADS * MLA_D_V
MLA_Q_BLOCK = 128

RET_HEADS = 4
RET_DK = 64
RET_DV = 128
RET_WIDTH = RET_HEADS * RET_DV
RET_CHUNK = 128

IN_SIZES = (
    HG_HEADS * HG_DK, HG_HEADS * HG_DK, HG_WIDTH, HG_WIDTH,
    MLA_D_CQ, MLA_D_C, MLA_D_ROPE, MLA_WIDTH,
    RET_HEADS * RET_DK, RET_HEADS * RET_DK, RET_WIDTH, RET_WIDTH,
    D_MODEL, D_MODEL, D_MODEL,
)
D_IN = sum(IN_SIZES)

kernel_name = "hybrid_hgrn2_mla_retention_block"

def rmsnorm(x, g=None):
    xf = x.astype(jnp.float32)
    y = xf * lax.rsqrt(jnp.mean(xf * xf, axis=-1, keepdims=True) + EPS)
    if g is not None:
        y = y * g.astype(jnp.float32)
    return y.astype(x.dtype)

def split_cols(p):
    parts, start = [], 0
    for s in IN_SIZES:
        parts.append(p[..., start:start + s])
        start += s
    return parts

def rope_tables(positions, dim):
    inv = ROPE_BASE ** (-jnp.arange(0, dim, 2, dtype=jnp.float32) / dim)
    ang = positions.astype(jnp.float32)[..., None] * inv
    return jnp.cos(ang), jnp.sin(ang)

def apply_rope(x, cos, sin):
    half = x.shape[-1] // 2
    x1, x2 = x[..., :half], x[..., half:]
    return jnp.concatenate([x1 * cos - x2 * sin, x2 * cos + x1 * sin], axis=-1)

def hgrn2_mixer(q_raw, f_raw, i_raw, lb, onorm_g):
    B, T, _ = q_raw.shape
    H, DK, DV, C = HG_HEADS, HG_DK, HG_DV, HG_CHUNK
    N = T // C
    q = jax.nn.silu(q_raw.astype(jnp.float32)) * (DK ** -0.5)
    z = f_raw.astype(jnp.float32)
    lb = lb.astype(jnp.float32)
    f = lb + (1.0 - lb) * jax.nn.sigmoid(z)
    log_f = jnp.log(jnp.maximum(f, LOG_FLOOR))
    k = (1.0 - lb) * jax.nn.sigmoid(-z)
    v = i_raw.astype(jnp.float32)

    def chunks(a, d):
        return a.reshape(B, N, C, H, d).transpose(1, 0, 3, 2, 4)

    causal = jnp.tril(jnp.ones((C, C), dtype=bool))[:, :, None]

    def step(S, inp):
        qc, kc, vc, gc = inp
        b = jnp.cumsum(gc, axis=2)
        diff = b[:, :, :, None, :] - b[:, :, None, :, :]
        decay = jnp.where(causal, jnp.exp(jnp.where(causal, diff, 0.0)), 0.0)
        attn = jnp.einsum('bhtd,bhsd,bhtsd->bhts', qc, kc, decay)
        o = jnp.einsum('bhts,bhsv->bhtv', attn, vc) + jnp.einsum('bhtd,bhdv->bhtv', qc * jnp.exp(b), S)
        b_last = b[:, :, -1:, :]
        S = jnp.exp(b_last[:, :, 0, :])[..., None] * S + jnp.einsum('bhsd,bhsv->bhdv', kc * jnp.exp(b_last - b), vc)
        return S, o

    S0 = jnp.zeros((B, H, DK, DV), jnp.float32)
    _, o = lax.scan(step, S0, (chunks(q, DK), chunks(k, DK), chunks(v, DV), chunks(log_f, DK)))
    o = o.transpose(1, 0, 3, 2, 4).reshape(B, T, H, DV)
    o = rmsnorm(o, onorm_g)
    return o.reshape(B, T, H * DV)

def mla_mixer(c_q, c_kv, k_rope_raw, g_cq, w_uq, g_ckv, w_ukv, cos, sin):
    B, T, _ = c_q.shape
    H, QB = MLA_HEADS, MLA_Q_BLOCK
    f32 = jnp.float32
    q = (rmsnorm(c_q.astype(f32), g_cq) @ w_uq.astype(f32)).reshape(B, T, H, MLA_D_NOPE + MLA_D_ROPE)
    q = q.transpose(0, 2, 1, 3)
    q_nope = q[..., :MLA_D_NOPE]
    q_rope = apply_rope(q[..., MLA_D_NOPE:], cos[:, None], sin[:, None])
    kv = (rmsnorm(c_kv.astype(f32), g_ckv) @ w_ukv.astype(f32)).reshape(B, T, H, MLA_D_NOPE + MLA_D_V)
    kv = kv.transpose(0, 2, 1, 3)
    k_nope, v = kv[..., :MLA_D_NOPE], kv[..., MLA_D_NOPE:]
    k_rope = apply_rope(k_rope_raw.astype(f32), cos, sin)
    scale = (MLA_D_NOPE + MLA_D_ROPE) ** -0.5
    nb = T // QB
    qn_b = q_nope.reshape(B, H, nb, QB, MLA_D_NOPE).transpose(2, 0, 1, 3, 4)
    qr_b = q_rope.reshape(B, H, nb, QB, MLA_D_ROPE).transpose(2, 0, 1, 3, 4)
    key_idx = jnp.arange(T)

    def block(args):
        qn, qr, start = args
        s = (jnp.einsum('bhqd,bhkd->bhqk', qn, k_nope) + jnp.einsum('bhqd,bkd->bhqk', qr, k_rope)) * scale
        q_idx = start + jnp.arange(QB)
        s = jnp.where(key_idx[None, :] <= q_idx[:, None], s, MASK_VALUE)
        p = jax.nn.softmax(s, axis=-1)
        return jnp.einsum('bhqk,bhkv->bhqv', p, v)

    o = lax.map(block, (qn_b, qr_b, jnp.arange(nb, dtype=jnp.int32) * QB))
    return o.transpose(1, 0, 3, 2, 4).reshape(B, T, H * MLA_D_V)

def retention_mixer(q_raw, k_raw, v_raw, cos, sin):
    B, T, _ = q_raw.shape
    H, DK, DV, C = RET_HEADS, RET_DK, RET_DV, RET_CHUNK
    N = T // C
    f32 = jnp.float32
    q = apply_rope(q_raw.astype(f32).reshape(B, T, H, DK).transpose(0, 2, 1, 3), cos[:, None], sin[:, None])
    k = apply_rope(k_raw.astype(f32).reshape(B, T, H, DK).transpose(0, 2, 1, 3), cos[:, None], sin[:, None]) * (DK ** -0.5)
    v = v_raw.astype(f32).reshape(B, T, H, DV).transpose(0, 2, 1, 3)
    log_gamma = jnp.log1p(-jnp.exp2(-5.0 - jnp.arange(H, dtype=f32)))
    qc = q.reshape(B, H, N, C, DK)
    kc = k.reshape(B, H, N, C, DK)
    vc = v.reshape(B, H, N, C, DV)
    pos = jnp.arange(C, dtype=f32)
    rel = pos[:, None] - pos[None, :]
    dmat = jnp.where(rel >= 0, jnp.exp(log_gamma[:, None, None] * jnp.maximum(rel, 0.0)), 0.0)
    scores = jnp.einsum('bhntd,bhnsd->bhnts', qc, kc) * dmat[None, :, None]
    o = jnp.einsum('bhnts,bhnsv->bhntv', scores, vc)
    k_dec = kc * jnp.exp(log_gamma[:, None] * (C - 1 - pos))[None, :, None, :, None]
    U = jnp.einsum('bhnsd,bhnsv->nbhdv', k_dec, vc)
    chunk_decay = jnp.exp(log_gamma * C)[None, :, None, None]

    def step(R, u):
        return chunk_decay * R + u, R

    _, R_prev = lax.scan(step, jnp.zeros((B, H, DK, DV), f32), U)
    q_dec = qc * jnp.exp(log_gamma[:, None] * (pos + 1.0))[None, :, None, :, None]
    o = o + jnp.einsum('bhntd,nbhdv->bhntv', q_dec, R_prev)
    o = o.reshape(B, H, T, DV).transpose(0, 2, 1, 3)
    o = rmsnorm(o)
    return o.reshape(B, T, H * DV)

def setup_inputs(seed: int = 0) -> dict:
    key = jax.random.key(seed)
    ks = jax.random.split(key, 20)
    f32 = jnp.float32

    def nrm(k, shape, fan_in):
        return jax.random.normal(k, shape, f32) * (fan_in ** -0.5)

    def gain(k, shape):
        return 1.0 + 0.01 * jax.random.normal(k, shape, f32)

    return {
        "x": jax.random.normal(ks[0], (BATCH, SEQ, D_MODEL), f32),
        "c": jax.random.normal(ks[1], (BATCH, D_MODEL), f32),
        "positions": jnp.broadcast_to(jnp.arange(SEQ, dtype=jnp.int32), (BATCH, SEQ)),
        "norm_g": gain(ks[2], (DEPTH, D_MODEL)),
        "w_mod": 0.5 * nrm(ks[3], (DEPTH, D_MODEL, 3 * D_MODEL), D_MODEL),
        "b_mod": 0.01 * jax.random.normal(ks[4], (DEPTH, 3 * D_MODEL), f32),
        "w_in": nrm(ks[5], (DEPTH, D_MODEL, D_IN), D_MODEL),
        "hg_lb_logits": 0.5 * jax.random.normal(ks[6], (DEPTH, HG_HEADS * HG_DK), f32),
        "hg_onorm_g": gain(ks[7], (DEPTH, HG_DV)),
        "mla_g_cq": gain(ks[8], (DEPTH, MLA_D_CQ)),
        "mla_w_uq": nrm(ks[9], (DEPTH, MLA_D_CQ, MLA_HEADS * (MLA_D_NOPE + MLA_D_ROPE)), MLA_D_CQ),
        "mla_g_ckv": gain(ks[10], (DEPTH, MLA_D_C)),
        "mla_w_ukv": nrm(ks[11], (DEPTH, MLA_D_C, MLA_HEADS * (MLA_D_NOPE + MLA_D_V)), MLA_D_C),
        "w_pa": nrm(ks[12], (DEPTH, HG_WIDTH, D_MODEL), HG_WIDTH),
        "w_pb": nrm(ks[13], (DEPTH, MLA_WIDTH, D_MODEL), MLA_WIDTH),
        "w_pc": nrm(ks[14], (DEPTH, RET_WIDTH, D_MODEL), RET_WIDTH),
        "w_out": nrm(ks[15], (DEPTH, D_MODEL, D_MODEL), D_MODEL),
        "final_g": gain(ks[16], (D_MODEL,)),
    }

def reference(x, c, positions, norm_g, w_mod, b_mod, w_in, hg_lb_logits, hg_onorm_g,
              mla_g_cq, mla_w_uq, mla_g_ckv, mla_w_ukv, w_pa, w_pb, w_pc, w_out, final_g):
    cos_m, sin_m = rope_tables(positions, MLA_D_ROPE)
    cos_r, sin_r = rope_tables(positions, RET_DK)
    p_lb = jax.nn.softmax(hg_lb_logits.astype(jnp.float32), axis=0)
    lower_bounds = jnp.cumsum(p_lb, axis=0) - p_lb[0:1]
    cond = jax.nn.silu(c)
    for l in range(DEPTH):
        mod = cond @ w_mod[l] + b_mod[l]
        shift = mod[:, None, :D_MODEL]
        scale = mod[:, None, D_MODEL:2 * D_MODEL]
        gate = mod[:, None, 2 * D_MODEL:]
        h = rmsnorm(x, norm_g[l]) * (1.0 + scale) + shift
        (a_q, a_f, a_i, a_g, b_cq, b_ckv, b_kr, b_g,
         c_q, c_k, c_v, c_g, m_a, m_b, m_c) = split_cols(h @ w_in[l])
        y_a = hgrn2_mixer(a_q, a_f, a_i, lower_bounds[l], hg_onorm_g[l]).astype(x.dtype) * jax.nn.silu(a_g)
        y_b = mla_mixer(b_cq, b_ckv, b_kr, mla_g_cq[l], mla_w_uq[l], mla_g_ckv[l], mla_w_ukv[l],
                        cos_m, sin_m).astype(x.dtype) * jax.nn.silu(b_g)
        y_c = retention_mixer(c_q, c_k, c_v, cos_r, sin_r).astype(x.dtype) * jax.nn.silu(c_g)
        merged = (jax.nn.sigmoid(m_a) * (y_a @ w_pa[l])
                  + jax.nn.sigmoid(m_b) * (y_b @ w_pb[l])
                  + jax.nn.sigmoid(m_c) * (y_c @ w_pc[l]))
        x = x + gate * (merged @ w_out[l])
    return rmsnorm(x, final_g)


_drawn_inputs = setup_inputs


def setup_inputs(seed=0):
    import zlib

    import numpy as np

    out = dict(_drawn_inputs(seed))
    spreads = {}
    factors = {'norm_g': 8.0,
     'b_mod': 5.592,
     'hg_lb_logits': 8.0,
     'hg_onorm_g': 8.0,
     'mla_g_cq': 8.0,
     'mla_w_uq': 2.892,
     'mla_g_ckv': 8.0,
     'final_g': 5.726}
    for name, (base, spread) in spreads.items():
        noise = np.random.default_rng([zlib.crc32(name.encode()), seed]).standard_normal(out[name].shape)
        drawn = base * np.exp(spread * noise) if base else spread * noise
        out[name] = __import__('jax').numpy.asarray(drawn.astype(out[name].dtype))
    for name, factor in factors.items():
        out[name] = (out[name] * factor).astype(out[name].dtype)
    return out
```

```python
from contextlib import ExitStack

import concourse.bass as bass
import numpy as np
from concourse import mybir

F32 = mybir.dt.float32
F32R = mybir.dt.float32r
BF16 = mybir.dt.bfloat16
I32 = mybir.dt.int32
U32 = mybir.dt.uint32
ACT = mybir.ActivationFunctionType
ALU = mybir.AluOpType
AX = mybir.AxisListType

P = 128
D_MODEL, SEQ, DEPTH = 1024, 512, 2
DT = D_MODEL // P
CH = SEQ // P
HG_HEADS, HG_DK = 4, 128
MLA_HEADS, NOPE, ROPE, MLA_DV, D_C, D_CQ = 8, 64, 32, 64, 256, 768
RET_HEADS, RET_DK, RET_DV = 4, 64, 128
CQT, CKT = D_CQ // P, D_C // P
EPS = 1e-6
MLA_SCALE = float(NOPE + ROPE) ** -0.5
TAU = 2.0 ** -60
EXP_CAP = 2.0 ** 60
TWO_PI = (6.28125, 0.0019340515136718750, 1.2556659146e-6)
LOG_FLOOR = 1e-20
ROUND = 12582912.0
PI_BELOW = 3.1415925
PRO_RING = 8
TABLE_SET = "natural_log_exp_and_others"
LINKS = {"act": 60, "dve": 99}
LEVELS = (64, 32, 16, 8, 4)
BASE = 4

OFF = {}
_at = 0
for _n, _s in (("a_q", 512), ("a_f", 512), ("a_i", 512), ("a_g", 512), ("b_cq", D_CQ), ("b_ckv", D_C), ("b_kr", ROPE),
               ("b_g", 512), ("c_q", 256), ("c_k", 256), ("c_v", 512), ("c_g", 512),
               ("m_a", D_MODEL), ("m_b", D_MODEL), ("m_c", D_MODEL)):
    OFF[_n] = _at
    _at += _s

MERGES = ("ma", "mb", "mc")

RING = 3
SLOT = DT * P


def merge_items(b):
    order = [("m", 0), ("m", 1), ("m", 2), ("p", 0), ("m", 3), ("m", 4), ("p", 1), ("m", 5), ("m", 6), ("p", 2),
             ("m", 7), ("p", 3)]
    return [(k + b, j) for k, j in order]


def tiles_of(item):
    kind = item[0]
    if kind in ("pa", "pb", "pc"):
        return [(4, P, 0, 2 * P), (4, P, P, 2 * P)]
    if kind == "mla":
        return [(CQT, NOPE + ROPE, 0, NOPE + ROPE), (CKT, P, CQT * (NOPE + ROPE), P)]
    if kind == "kr":
        return [(DT, NOPE + ROPE, 0, NOPE + ROPE)]
    return [(DT, P, 0, P)]


def elements_of(item):
    return {"pa": 1024, "pb": 1024, "pc": 1024, "mla": CQT * 96 + CKT * P, "kr": DT * 96}.get(item[0], DT * P)


def build_schedule():
    s = [("norm",)]

    def item(kind, j):
        s.append(("item", kind, j))

    for h in range(HG_HEADS):
        item("f", h)
        if h:
            s += [("hg_lv", h - 1, 4), ("hg_lv", h - 1, 5)]
        item("q", h)
        if h:
            s += [("hg_lv", h - 1, 6), ("hg_lv", h - 1, 7)]
        item("i", h)
        if h:
            s += [("hg_pv", h - 1)]
        s += [("hg_lv", h, 0), ("hg_lv", h, 1)]
        item("g", h)
        if h:
            s += [("hg_out", h - 1)]
        s += [("hg_lv", h, 2), ("hg_lv", h, 3)]
    h = HG_HEADS - 1
    item("cq", 0)
    s += [("hg_lv", h, 4), ("hg_lv", h, 5)]
    item("cq", 1)
    s += [("hg_lv", h, 6), ("hg_lv", h, 7)]
    item("cq", 2)
    s += [("hg_pv", h)]
    item("cq", 3)
    s += [("hg_out", h)]
    item("cq", 4)
    item("cq", 5)
    s.append(("cq_norm",))
    item("ckv", 0)
    item("ckv", 1)
    s.append(("ckv_norm",))
    item("kr", 0)
    s.append(("kr_rope",))
    for k, j in merge_items("a"):
        item(k, j)
    item("mla", 0)
    s.append(("mla_qk", 0))
    item("bg", 0)
    for h in range(MLA_HEADS):
        s += [("mla_s", h, 0), ("mla_s", h, 1)]
        if h + 1 < MLA_HEADS:
            item("mla", h + 1)
        else:
            item("rq", 0)
        s += [("mla_t", h, 0), ("mla_t", h, 1), ("mla_s", h, 2), ("mla_s", h, 3)]
        if h + 1 < MLA_HEADS:
            s.append(("mla_qk", h + 1))
        else:
            s.append(("ret_rope", "rq", 0))
        if h % 2 == 1 and h + 1 < MLA_HEADS:
            item("bg", (h + 1) // 2)
        if h + 1 == MLA_HEADS:
            item("rq", 1)
        s += [("mla_t", h, 2), ("mla_t", h, 3), ("mla_pv", h)]
        if h + 1 == MLA_HEADS:
            s.append(("ret_rope", "rq", 1))
    item("rk", 0)
    s.append(("ret_rope", "rk", 0))
    item("rk", 1)
    s.append(("ret_rope", "rk", 1))
    for h in range(RET_HEADS):
        item("rv", h)
        s.append(("ret_v", h))
    mb = merge_items("b")
    for h in range(RET_HEADS):
        s += [("ret_s", h, 0), ("ret_s", h, 1)]
        item(*mb[3 * h])
        s += [("ret_s", h, 2), ("ret_s", h, 3)]
        item("cg", h)
        s += [("ret_pv", h)]
        item(*mb[3 * h + 1])
        s += [("ret_out", h)]
        item(*mb[3 * h + 2])
    for k, j in merge_items("c"):
        item(k, j)
    for j in range(DT):
        item("wo", j)
    s.append(("end",))
    return s


SCHEDULE = build_schedule()
ITEMS = [s[1:] for s in SCHEDULE if s[0] == "item"]
N_ITEMS = len(ITEMS)
ITEM_AT = {it: n for n, it in enumerate(ITEMS)}
ITEM_BASE = np.concatenate([[0], np.cumsum([elements_of(it) * P for it in ITEMS])]).astype(int).tolist()
assert N_ITEMS % RING == 0

STREAM = ("st0", "st1")
BANKS = ("st0", "st1", "s0", "s1", "w0", "w1", "o", "misc")


def build_uses():
    count = dict.fromkeys(BANKS, 0)
    uses = {}

    def use(bank, key):
        uses[key] = (bank, count[bank])
        count[bank] += 1

    out = 0
    for s in SCHEDULE:
        kind = s[0]
        if kind == "norm":
            use("misc", ("ssq",))
        elif kind == "item":
            for t in range(len(tiles_of(s[1:]))):
                use(STREAM[out % 2], (s[1:], t))
                out += 1
            if s[1] == "i":
                use("misc", ("hg_v", s[2]))
        elif kind == "hg_lv":
            if 1 <= s[2] <= 6:
                use(("s0", "s1")[(s[2] - 1) % 2], ("lv", s[1], s[2] - 1))
            if s[2] == 7:
                use("w0", ("cross0", s[1]))
                use("w1", ("cross1", s[1]))
        elif kind in ("hg_pv", "ret_pv"):
            use("o", (kind, s[1]))
        elif kind in ("hg_out", "ret_out", "cq_norm", "ckv_norm", "ret_rope", "kr_rope", "ret_v"):
            use("misc", s)
        elif kind == "mla_qk":
            use("misc", ("mla_swap", s[1]))
            use("misc", ("mla_v", s[1]))
        elif kind == "mla_s":
            use(("s0", "s1")[s[2] % 2], s)
        elif kind == "mla_t":
            use(("w0", "w1")[s[2] % 2], s)
        elif kind == "mla_pv":
            use("o", s)
        elif kind == "ret_s":
            use(("s0", "s1")[s[2] % 2], s)
        elif kind == "mod_sum":
            use("misc", s)
    return uses, count


MOD_W = 512
MOD_SECTIONS = D_MODEL * 3 // MOD_W


def add_mod_steps():
    steps = []
    for sec in range(MOD_SECTIONS):
        for k in range(DT):
            steps.append(("mod_acc", sec, k))
        steps.append(("mod_sum", sec))
    out = []
    n = 0
    total = N_ITEMS - 12
    for s in SCHEDULE:
        out.append(s)
        if s[0] == "item":
            n += 1
            while steps and len(steps) > (total - n) * (MOD_SECTIONS * (DT + 1)) / total:
                out.append(steps.pop(0))
    assert not steps
    return out


SCHEDULE = add_mod_steps()
USES, BANK_USES = build_uses()

CUR = {}
_at = 0
for _n, _s in (("b_gate", DT), ("logits", DEPTH * HG_HEADS), ("sel", DEPTH), ("onorm", 1), ("g_cq", CQT), ("g_ckv", CKT)):
    CUR[_n] = (_at, _at + _s)
    _at += _s
N_CUR = _at
NXT = {"norm_g": (0, DT), "b_shift": (DT, 2 * DT), "b_scale": (2 * DT, 3 * DT)}
N_NXT = 3 * DT
CST = {}
_at = 0
for _n, _s in (("ident", P), ("ones", P), ("perm_mla", P), ("perm_ret", P), ("m64", P), ("m32", P), ("m16", P),
               ("m8", P), ("m4", P), ("mbase", P), ("reset", SEQ), ("neg", P), ("inv_mla", 1), ("inv_ret", 1),
               ("eps", 1), ("one", 1), ("half_pi", 1), ("c", DT), ("final_g", DT)):
    CST[_n] = (_at, _at + _s)
    _at += _s
N_CST = _at



def bank_of(key):
    return USES[key][0]


GATES = HG_HEADS * 2 + MLA_HEADS // 2 + RET_HEADS
PAIRS = MLA_HEADS // 2
PER_LAYER = {
    **{f"{s}_{b}": n for s in ("full", "free") for b, n in BANK_USES.items()},
    **{f"raw_in{i}": 16 * (N_ITEMS // RING) for i in range(RING)},
    **{f"mod_in{i}": 16 * (MOD_SECTIONS * DT // 2) for i in range(2)},
    "mod_done": MOD_SECTIONS * DT, "params_in": 32, "decay_in": 16, "lb_d_ready": 1, "lb_e_ready": 1,
    "w_hi_ready": N_ITEMS, "w_lo_ready": N_ITEMS,
    "sq_sum_ready": 1, "norm_t": DT, "norm_hi": DT, "h_ready": DT, "x_sq": DT, "x_sum": DT - 1,
    "mg_t": DT, "mg_hi_ready": DT, "mg_ready": DT,
    "rstd_ready": 3 + HG_HEADS + RET_HEADS + MLA_HEADS,
    "gate_exp": GATES, "gate_sig": GATES, "gate_cap": GATES + 3 * DT, "sigma_ready": 3 * DT,
    "hz_ln": HG_HEADS, "hz_s": HG_HEADS, "hz_f": HG_HEADS, "hz_l": HG_HEADS, "b_ready": HG_HEADS,
    "d_ready": 7 * HG_HEADS, "e_ready": 7 * HG_HEADS, "x_built": 7 * HG_HEADS,
    "o_sq_ready": HG_HEADS + RET_HEADS,
    "y_t_ready": HG_HEADS + PAIRS + RET_HEADS, "y_hi_ready": HG_HEADS + PAIRS + RET_HEADS,
    "y_ready": HG_HEADS + PAIRS + RET_HEADS,
    "cq_sq": CQT + CKT, "cq_sum": CQT + CKT, "cqn_t": CQT + CKT, "cqn_hi": CQT + CKT, "cqn_ready": CQT + CKT,
    "q_ready": MLA_HEADS, "k_ready": MLA_HEADS, "p_max": CH * MLA_HEADS, "ret_qk_ready": 4,
    "act_link": LINKS["act"], "dve_link": LINKS["dve"],
}


class Counter:

    def __init__(self, eng, layer, per_layer):
        self.eng, self.layer, self.per_layer = eng, layer, per_layer
        self.asked, self.own = {}, {}
        self.base, self.value = {}, eng.alloc_register(name="wait_value")

    def at(self, sem, k):
        self.asked[id(sem)] = max(k, self.asked.get(id(sem), 0))
        n = self.per_layer[id(sem)]
        if n not in self.base:
            self.base[n] = self.eng.alloc_register(name=f"layer_times_{n}")
            self.eng.reg_mul(self.base[n], self.layer, n)
        self.eng.reg_add(self.value, self.base[n], k)
        return self.value

    def new(self, sem, k):
        return self.asked.get(id(sem), 0) < k

    def use(self, banks, key):
        b, k = USES[key]
        return self.at(banks[b], k + 1)

    def made(self, sem):
        self.own[id(sem)] = self.own.get(id(sem), 0) + 1
        return self.at(sem, self.own[id(sem)])


def build(nc, x_t, positions, cst, decay, params_cur, params_nxt, w_stream, w_mod, w_mod_first, out_t):
    ctx = ExitStack()
    with ctx:
        def sb(name, shape, dt=F32):
            return ctx.enter_context(nc.sbuf_tensor(name, shape, dt))

        def sem(name):
            return ctx.enter_context(nc.semaphore(name))

        x = sb("x", [P, DT, SEQ])
        h_hi = sb("h_hi", [P, DT, SEQ], F32R)
        h_lo = sb("h_lo", [P, DT, SEQ], F32R)
        raw = sb("raw", [P, RING, SLOT])
        w_hi = sb("w_hi", [P, RING, SLOT], F32R)
        w_lo = sb("w_lo", [P, RING, SLOT], F32R)
        mod_w = sb("mod_w", [P, 2, MOD_W])
        mod_acc = sb("mod_acc", [P, MOD_W])
        cs = sb("cs", [P, N_CST])
        cos_mla, sin_mla = sb("cos_mla", [P, SEQ]), sb("sin_mla", [P, SEQ])
        cos_ret, sin_ret = sb("cos_ret", [P, SEQ]), sb("sin_ret", [P, SEQ])
        ident_bf, neg_bf = sb("ident_bf", [P, P], BF16), sb("neg_bf", [P, P], BF16)
        v_ones = sb("v_ones", [P, 2, CH, 3 * MLA_DV])
        rstd = sb("rstd", [P, SEQ])
        gate_t = sb("gate_t", [P, SEQ])
        t1, t2, y_t = sb("t1", [P, SEQ]), sb("t2", [P, SEQ]), sb("y_t", [P, SEQ])
        sq_t, sq_sum, o_sq = sb("sq_t", [P, SEQ]), sb("sq_sum", [P, SEQ]), sb("o_sq", [P, SEQ])
        cur = sb("cur", [P, N_CUR])
        nxt = sb("nxt", [P, N_NXT])
        shift, scale_g, gate = sb("shift", [P, DT]), sb("scale_g", [P, DT]), sb("gate", [P, DT])
        cond, cond_t = sb("cond", [P, DT]), sb("cond_t", [P, DT])
        lb, one_lb = sb("lb", [P, HG_HEADS]), sb("one_lb", [P, HG_HEADS])
        lb_e = sb("lb_e", [P, DEPTH, HG_HEADS])
        lb_t = sb("lb_t", [P, HG_HEADS])
        centre = sb("centre", [P, SEQ // BASE])
        g_last = sb("g_last", [P, CH])
        carry = sb("carry", [P, 1])
        row_max, neg_max = sb("row_max", [P, CH]), sb("neg_max", [P, CH])

        arena = nc.sbuf_base + (-nc.sbuf_base) % 64
        KB = 1024

        def at(name, offset, shape, dt=F32):
            return nc.alloc_sbuf_tensor_at(name, shape, dt, offset=arena + offset)

        hg_q, hg_k, hg_b = at("hg_q", 0, [P, 2, SEQ]), at("hg_k", 4 * KB, [P, 2, SEQ]), at("hg_b", 8 * KB, [P, 2, SEQ])
        hg_e, hg_x = at("hg_e", 12 * KB, [P, 2, SEQ]), at("hg_x", 16 * KB, [P, 2, SEQ])
        hg_at = at("hg_at", 20 * KB, [P, CH, SEQ])
        hg_kd = at("hg_kd", 28 * KB, [P, 3 * P])
        hg_qc = at("hg_qc", 64 * KB, [P, 3, 3 * P])
        hg_vt = at("hg_vt", 69 * KB, [P, SEQ])
        hg_v = at("hg_v", 71 * KB, [P, 2, CH, P])
        hg_g = at("hg_g", 75 * KB, [P, 2, SEQ])
        hz_a, hz_b, hz_c = at("hz_a", 79 * KB, [P, SEQ]), at("hz_b", 81 * KB, [P, SEQ]), at("hz_c", 83 * KB, [P, SEQ])
        cq_hi, cq_lo = at("cq_hi", 0, [P, CQT, SEQ], F32R), at("cq_lo", 12 * KB, [P, CQT, SEQ], F32R)
        ckv_hi, ckv_lo = at("ckv_hi", 24 * KB, [P, CKT, SEQ], F32R), at("ckv_lo", 28 * KB, [P, CKT, SEQ], F32R)
        cq_raw, ckv_raw = at("cq_raw", 32 * KB, [P, CQT, SEQ]), at("ckv_raw", 44 * KB, [P, CKT, SEQ])
        mla_q, mla_kv = at("mla_q", 64 * KB, [P, 2, SEQ]), at("mla_kv", 68 * KB, [P, 2, SEQ])
        mla_p, mla_pt = at("mla_p", 72 * KB, [P, 2, SEQ]), at("mla_pt", 76 * KB, [P, CH, SEQ])
        mla_g = at("mla_g", 84 * KB, [P, 2, SEQ])
        k_rope = at("k_rope", 90 * KB, [P, SEQ])
        ret_q, ret_k = at("ret_q", 0, [P, 2, SEQ]), at("ret_k", 4 * KB, [P, 2, SEQ])
        ret_v = at("ret_v", 8 * KB, [P, RET_HEADS, CH, P])
        ret_sc = at("ret_sc", 16 * KB, [P, CH, SEQ])
        ret_decay = at("ret_decay", 24 * KB, [P, RET_HEADS, SEQ])
        yc_hi, yc_lo = at("yc_hi", 64 * KB, [P, CH, SEQ], F32R), at("yc_lo", 72 * KB, [P, CH, SEQ], F32R)
        ret_vt, ret_g = at("ret_vt", 80 * KB, [P, SEQ]), at("ret_g", 82 * KB, [P, SEQ])
        merged = at("merged", 32 * KB, [P, DT, SEQ])
        y_hi, y_lo = at("y_hi", 48 * KB, [P, CH, SEQ], F32R), at("y_lo", 56 * KB, [P, CH, SEQ], F32R)
        sigma = at("sigma", 84 * KB, [P, 3, SEQ])
        arena_end = arena + 92 * KB
        assert arena_end <= nc.sbuf_usable_end, (arena_end, nc.sbuf_usable_end)
        mg_hi, mg_lo = at("mg_hi", 0, [P, DT, SEQ], F32R), at("mg_lo", 16 * KB, [P, DT, SEQ], F32R)
        pro_w = at("pro_w", 0, [P, PRO_RING, D_MODEL])
        pro_acc = at("pro_acc", 32 * KB, [P, 2 * D_MODEL])
        pos_i = at("pos_i", 40 * KB, [P, SEQ], I32)
        pos_f, ang, turn = at("pos_f", 42 * KB, [P, SEQ]), at("ang", 44 * KB, [P, SEQ]), at("turn", 46 * KB, [P, SEQ])
        red = at("red", 48 * KB, [P, 4, SEQ])
        o_t = at("o_t", 0, [P, DT, SEQ])

        def c(name):
            a, b = CST[name]
            return cs[:, a:b]

        def pc(name):
            a, b = CUR[name]
            return cur[:, a:b]

        def pn(name):
            a, b = NXT[name]
            return nxt[:, a:b]

        def diagonal(t):
            a = t[:, :, 0:P]
            steps = [list(v) for v in a.ap]
            steps[-2][0] += P
            return bass.AP(tensor=a.tensor, offset=a.offset, ap=steps)

        ident, ones, eps, one = c("ident"), c("ones"), c("eps"), c("one")

        bank = {n: ctx.enter_context(nc.psum_tensor("ps_" + n, [P, SEQ], F32)) for n in BANKS}

        per_layer = {}

        def signal(name):
            s = sem(name)
            per_layer[id(s)] = PER_LAYER[name]
            return s

        full = {n: signal("full_" + n) for n in BANKS}
        free = {n: signal("free_" + n) for n in BANKS}
        raw_in = [signal(f"raw_in{i}") for i in range(RING)]
        mod_in = [signal(f"mod_in{i}") for i in range(2)]
        w_hi_ready = signal("w_hi_ready")
        w_lo_ready = signal("w_lo_ready")
        sq_sum_ready = signal("sq_sum_ready")
        act_link, dve_link = signal("act_link"), signal("dve_link")
        rstd_ready = signal("rstd_ready")
        norm_t, norm_hi, h_ready = signal("norm_t"), signal("norm_hi"), signal("h_ready")
        gate_exp, gate_cap, gate_sig, sigma_ready = (signal(n) for n in ("gate_exp", "gate_cap", "gate_sig", "sigma_ready"))
        hz_ln, hz_s, hz_f, hz_l = (signal(n) for n in ("hz_ln", "hz_s", "hz_f", "hz_l"))
        b_ready, d_ready, e_ready, x_built = (signal(n) for n in ("b_ready", "d_ready", "e_ready", "x_built"))
        o_sq_ready, y_t_ready, y_hi_ready, y_ready = (signal(n) for n in ("o_sq_ready", "y_t_ready", "y_hi_ready", "y_ready"))
        cq_sq, cq_sum, cqn_t, cqn_hi, cqn_ready = (signal(n) for n in ("cq_sq", "cq_sum", "cqn_t", "cqn_hi", "cqn_ready"))
        q_ready, k_ready, p_max = (signal(n) for n in ("q_ready", "k_ready", "p_max"))
        ret_qk_ready, decay_in = signal("ret_qk_ready"), signal("decay_in")
        mg_t, mg_hi_ready, mg_ready = (signal(n) for n in ("mg_t", "mg_hi_ready", "mg_ready"))
        x_sq, x_sum = signal("x_sq"), signal("x_sum")
        params_in, lb_d_ready, lb_e_ready = (signal(n) for n in ("params_in", "lb_d_ready", "lb_e_ready"))
        mod_done = signal("mod_done")
        names = ("const_in", "x_in", "pos_in", "par_in", "cond_e", "pro_link", "pro_mod_done", "pro_mod_sum", "pro_mod_read",
                 "angles", "tables", "pro_sq", "pro_sum", "fin_sum", "fin_link", "fin_rstd", "fin_out", "stored")
        (const_in, x_in, pos_in, par_in, cond_e, pro_link, pro_mod_done, pro_mod_sum, pro_mod_read, angles, tables, pro_sq,
         pro_sum, fin_sum, fin_link, fin_rstd, fin_out, stored) = (sem(n) for n in names)
        pro_in = [sem(f"pro_in{i}") for i in range(PRO_RING)]

        block = ctx.enter_context(nc.Block())

        @block.sync
        def _(sp):
            sp.dma_start(cs[:], cst).then_inc(const_in, 16)
            for j in range(0, DT, 2):
                sp.dma_start(x[:, j:j + 2, :], x_t[:, j:j + 2, :]).then_inc(x_in, 16)
            with sp.Fori(0, DEPTH) as layer:
                e = Counter(sp, layer, per_layer)
                for i, it in enumerate(ITEMS):
                    n = elements_of(it)
                    sp.wait_ge(w_lo_ready, e.at(w_lo_ready, i + 1))
                    src = w_stream[layer, ITEM_BASE[i]:ITEM_BASE[i] + P * n].rearrange("(p n) -> p n", p=P)
                    sp.dma_start(raw[:, i % RING, 0:n], src).then_inc(raw_in[i % RING], 16)
            for j in range(DT):
                sp.wait_ge(fin_out, j + 1)
                sp.dma_start(out_t[:, j, :], o_t[:, j, :]).then_inc(stored, 16)
            sp.wait_ge(stored, 16 * DT)

        @block.gpsimd
        def _(pool):
            pool.sem_inc(w_lo_ready, RING)
            with pool.Fori(0, DEPTH) as layer:
                e = Counter(pool, layer, per_layer)
                for i, it in enumerate(ITEMS):
                    n = elements_of(it)
                    pool.wait_ge(w_hi_ready, e.at(w_hi_ready, i + 1))
                    nc.gpsimd.tensor_tensor(w_lo[:, i % RING, 0:n], raw[:, i % RING, 0:n],
                                            w_hi[:, i % RING, 0:n].bitcast(F32), ALU.subtract).then_inc(w_lo_ready, 1)

        @block.tensor
        def _(pe):
            pe.wait_ge(const_in, 16)
            pe.wait_ge(pro_mod_done, 2 * DT)
            for j in range(2 * DT):
                last = nc.tensor.matmul(bank["misc"][:, j:j + 1], pro_acc[:, j * P:(j + 1) * P], ones[:, 0:1],
                                        start=True, stop=True)
            last.then_inc(pro_mod_sum, 1)
            with pe.Fori(0, DEPTH) as layer:
                e = Counter(pe, layer, per_layer)

                def take(key):
                    b, k = USES[key]
                    if k > 0:
                        if e.new(free[b], k):
                            pe.wait_ge(free[b], e.at(free[b], k))
                    return bank[b]

                def done(ins, key):
                    ins.then_inc(full[bank_of(key)], 1)

                def moving(kind, t, k):
                    if kind == "pa":
                        if e.new(y_ready, k + 1):
                            pe.wait_ge(y_ready, e.at(y_ready, k + 1))
                        return y_hi[:, k, :], y_lo[:, k, :]
                    if kind == "pb":
                        if e.new(y_ready, CH + k + 1):
                            pe.wait_ge(y_ready, e.at(y_ready, CH + k + 1))
                        return y_hi[:, k, :], y_lo[:, k, :]
                    if kind == "pc":
                        if e.new(y_ready, 2 * CH + k + 1):
                            pe.wait_ge(y_ready, e.at(y_ready, 2 * CH + k + 1))
                        return yc_hi[:, k, :], yc_lo[:, k, :]
                    if kind == "mla" and t == 0:
                        if e.new(cqn_ready, k + 1):
                            pe.wait_ge(cqn_ready, e.at(cqn_ready, k + 1))
                        return cq_hi[:, k, :], cq_lo[:, k, :]
                    if kind == "mla":
                        if e.new(cqn_ready, CQT + k + 1):
                            pe.wait_ge(cqn_ready, e.at(cqn_ready, CQT + k + 1))
                        return ckv_hi[:, k, :], ckv_lo[:, k, :]
                    if kind == "wo":
                        if e.new(mg_ready, k + 1):
                            pe.wait_ge(mg_ready, e.at(mg_ready, k + 1))
                        return mg_hi[:, k, :], mg_lo[:, k, :]
                    if e.new(h_ready, k + 1):
                        pe.wait_ge(h_ready, e.at(h_ready, k + 1))
                    return h_hi[:, k, :], h_lo[:, k, :]

                def item(it):
                    i = ITEM_AT[it]
                    pe.wait_ge(w_lo_ready, e.at(w_lo_ready, RING + i + 1))
                    for t, (nk, m, first, step) in enumerate(tiles_of(it)):
                        dst = take((it, t))
                        for k in range(nk):
                            hi, lo = moving(it[0], t, k)
                            a = first + k * step
                            wh, wl = w_hi[:, i % RING, a:a + m], w_lo[:, i % RING, a:a + m]
                            nc.tensor.matmul(dst[0:m, :], wh, hi, start=(k == 0), stop=False)
                            nc.tensor.matmul(dst[0:m, :], wh, lo, start=False, stop=False)
                            last = nc.tensor.matmul(dst[0:m, :], wl, hi, start=False, stop=(k == nk - 1))
                        done(last, (it, t))

                def transposes(key, src):
                    dst = take(key)
                    for k in range(CH):
                        last = nc.tensor.transpose(dst[:, k * P:(k + 1) * P], src(k), ident)
                    done(last, key)

                def swap_halves(key, perm, src, rows):
                    dst = take(key)
                    done(nc.tensor.matmul(dst[0:rows, :], perm[0:rows, 0:rows], src, start=True, stop=True), key)

                def column_sums(key, src):
                    dst = take(key)
                    done(nc.tensor.matmul(dst[:], ones, src, start=True, stop=True), key)

                def weighted_values(key, values, weights):
                    dst = take(key)
                    for k in range(CH):
                        last = nc.tensor.matmul(dst[:, k * P:], values(k), weights[:, k, k * P:],
                                                start=(k == 0), stop=(k == CH - 1))
                    done(last, key)

                for s in SCHEDULE:
                    kind = s[0]
                    if kind == "norm":
                        pe.wait_ge(sq_sum_ready, e.at(sq_sum_ready, 1))
                        column_sums(("ssq",), sq_sum[:])
                    elif kind == "item":
                        item(s[1:])
                        if s[1] == "i":
                            pe.wait_ge(free[bank_of((s[1:], 0))], e.use(free, (s[1:], 0)))
                            transposes(("hg_v", s[2]), lambda k: hg_vt[:, k * P:(k + 1) * P])
                    elif kind == "hg_lv" and 1 <= s[2] <= 6:
                        h, n = s[1], s[2] - 1
                        pe.wait_ge(x_built, e.at(x_built, 7 * h + n + 1))
                        dst = take(("lv", h, n))
                        left, right = (hg_x[:, n % 2, :], hg_x[:, n % 2, :]) if n < 5 else (hg_x[:, 0, :], hg_x[:, 1, :])
                        for k in range(CH):
                            r = slice(k * P, (k + 1) * P)
                            last = nc.tensor.matmul(dst[:, r], left[:, r], right[:, r], start=True, stop=True)
                        done(last, ("lv", h, n))
                    elif kind == "hg_lv" and s[2] == 7:
                        h = s[1]
                        pe.wait_ge(x_built, e.at(x_built, 7 * h + 7))
                        d0 = take(("cross0", h))
                        nc.tensor.matmul(d0[:, 0:3 * P], hg_kd[:, 0:P], hg_qc[:, 0, :], start=True, stop=True)
                        done(nc.tensor.matmul(d0[:, 3 * P:], hg_kd[:, 2 * P:3 * P], hg_qc[:, 2, 0:P], start=True, stop=True),
                             ("cross0", h))
                        d1 = take(("cross1", h))
                        done(nc.tensor.matmul(d1[:, 0:2 * P], hg_kd[:, P:2 * P], hg_qc[:, 1, 0:2 * P], start=True, stop=True),
                             ("cross1", h))
                    elif kind == "hg_pv":
                        h = s[1]
                        pe.wait_ge(free[bank_of(("hg_v", h))], e.use(free, ("hg_v", h)))
                        pe.wait_ge(free[bank_of(("lv", h, 4))], e.use(free, ("lv", h, 4)))
                        pe.wait_ge(free[bank_of(("lv", h, 5))], e.use(free, ("lv", h, 5)))
                        pe.wait_ge(free[bank_of(("cross0", h))], e.use(free, ("cross0", h)))
                        pe.wait_ge(free[bank_of(("cross1", h))], e.use(free, ("cross1", h)))
                        weighted_values(s, lambda k: hg_v[:, h % 2, k, :], hg_at)
                    elif kind in ("hg_out", "ret_out"):
                        pe.wait_ge(o_sq_ready, e.at(o_sq_ready, (0 if kind == "hg_out" else HG_HEADS) + s[1] + 1))
                        column_sums(s, o_sq[:])
                    elif kind in ("cq_norm", "ckv_norm"):
                        pe.wait_ge(cq_sum, e.at(cq_sum, CQT if kind == "cq_norm" else CQT + CKT))
                        column_sums(s, sq_sum[:])
                    elif kind == "kr_rope":
                        pe.wait_ge(free[bank_of((("kr", 0), 0))], e.use(free, (("kr", 0), 0)))
                        swap_halves(s, c("perm_mla"), k_rope[0:96, :], 96)
                    elif kind == "ret_rope":
                        pe.wait_ge(free[bank_of((s[1:], 0))], e.use(free, (s[1:], 0)))
                        swap_halves(s, c("perm_ret"), (ret_q if s[1] == "rq" else ret_k)[:, s[2], :], P)
                    elif kind == "ret_v":
                        pe.wait_ge(free[bank_of((("rv", s[1]), 0))], e.use(free, (("rv", s[1]), 0)))
                        transposes(s, lambda k: ret_vt[:, k * P:(k + 1) * P])
                    elif kind == "mla_qk":
                        h = s[1]
                        pe.wait_ge(free[bank_of((("mla", h), 0))], e.use(free, (("mla", h), 0)))
                        swap_halves(("mla_swap", h), c("perm_mla"), mla_q[0:96, h % 2, :], 96)
                        pe.wait_ge(free[bank_of((("mla", h), 1))], e.use(free, (("mla", h), 1)))
                        transposes(("mla_v", h), lambda k: mla_kv[:, h % 2, k * P:(k + 1) * P])
                    elif kind == "mla_s":
                        h, qi = s[1:]
                        if e.new(q_ready, h + 1):
                            pe.wait_ge(q_ready, e.at(q_ready, h + 1))
                        if e.new(k_ready, h + 1):
                            pe.wait_ge(k_ready, e.at(k_ready, h + 1))
                        dst = take(s)
                        w = (qi + 1) * P
                        nc.tensor.matmul(dst[:, 0:w], mla_q[0:96, h % 2, qi * P:w], mla_kv[0:96, h % 2, 0:w],
                                         start=True, stop=False)
                        done(nc.tensor.matmul(dst[:, qi * P:w], ident_bf[:], neg_bf[:], start=False, stop=True), s)
                    elif kind == "mla_t":
                        h, qi = s[1:]
                        pe.wait_ge(free[bank_of(("mla_s", h, qi))], e.use(free, ("mla_s", h, qi)))
                        dst = take(s)
                        for k in range(qi + 1):
                            last = nc.tensor.transpose(dst[:, k * P:(k + 1) * P], mla_p[:, qi % 2, k * P:(k + 1) * P], ident)
                        done(last, s)
                    elif kind == "mla_pv":
                        h = s[1]
                        pe.wait_ge(free[bank_of(("mla_t", h, 2))], e.use(free, ("mla_t", h, 2)))
                        pe.wait_ge(free[bank_of(("mla_t", h, 3))], e.use(free, ("mla_t", h, 3)))
                        pe.wait_ge(free[bank_of(("mla_v", h))], e.use(free, ("mla_v", h)))
                        a = 0 if h % 2 == 0 else MLA_DV
                        weighted_values(s, lambda k: v_ones[:, (h // 2) % 2, k, a:a + P], mla_pt)
                    elif kind == "ret_s":
                        h, k = s[1:]
                        if e.new(ret_qk_ready, 4):
                            pe.wait_ge(ret_qk_ready, e.at(ret_qk_ready, 4))
                        r = slice(RET_DK * (h % 2), RET_DK * (h % 2) + RET_DK)
                        dst = take(s)
                        done(nc.tensor.matmul(dst[:, 0:SEQ - k * P], ret_k[r, h // 2, k * P:(k + 1) * P],
                                              ret_q[r, h // 2, k * P:], start=True, stop=True), s)
                    elif kind == "ret_pv":
                        h = s[1]
                        pe.wait_ge(free[bank_of(("ret_s", h, 2))], e.use(free, ("ret_s", h, 2)))
                        pe.wait_ge(free[bank_of(("ret_s", h, 3))], e.use(free, ("ret_s", h, 3)))
                        pe.wait_ge(free[bank_of(("ret_v", h))], e.use(free, ("ret_v", h)))
                        weighted_values(s, lambda k: ret_v[:, h, k, :], ret_sc)
                    elif kind == "mod_sum":
                        pe.wait_ge(mod_done, e.at(mod_done, (s[1] + 1) * DT))
                        dst = take(s)
                        for j in range(MOD_W // P):
                            last = nc.tensor.matmul(dst[:, j:j + 1], mod_acc[:, j * P:(j + 1) * P], ones[:, 0:1],
                                                    start=True, stop=True)
                        done(last, s)
            pe.wait_ge(sq_sum_ready, DEPTH + 1)
            nc.tensor.matmul(bank["misc"][:], ones, sq_sum[:], start=True, stop=True).then_inc(fin_sum, 1)

        @block.scalar
        def _(act):
            A = nc.scalar.activation
            act.dma_start(nxt[:], params_nxt[DEPTH]).then_inc(par_in, 16)
            act.dma_start(pos_i[:], positions[0:1, :].to_broadcast([P, SEQ])).then_inc(pos_in, 16)
            for n in range(2 * DT):
                if n >= PRO_RING:
                    act.wait_ge(pro_mod_done, n - PRO_RING + 1)
                act.dma_start(pro_w[:, n % PRO_RING, :], w_mod_first[n]).then_inc(pro_in[n % PRO_RING], 16)
                if n == PRO_RING - 1:
                    act.wait_ge(const_in, 16)
                    A(cond_t[:], c("c"), ACT.Exp, scale=-1.0).then_inc(cond_e, 1)
            act.wait_ge(x_in, 16 * (DT // 2))
            for j in range(DT):
                if j >= 2:
                    act.wait_ge(pro_sum, j - 1)
                A((sq_t, o_sq)[j % 2][:], x[:, j, :], ACT.Square).then_inc(pro_sq, 1)
            for n, dst in enumerate((sin_mla, cos_mla, sin_ret, cos_ret)):
                act.wait_ge(angles, n + 1)
                A(dst[:], red[:, n, :], ACT.Sin).then_inc(tables, 1)
            act.preload_act_table_set(TABLE_SET)
            with act.Fori(0, DEPTH) as layer:
                e = Counter(act, layer, per_layer)
                silu_before = []
                gated = []

                def split(i):
                    if i >= N_ITEMS:
                        return
                    n = elements_of(ITEMS[i])
                    act.wait_ge(raw_in[i % RING], e.at(raw_in[i % RING], 16 * (i // RING + 1)))
                    if i >= RING:
                        before = (ITEMS[i - RING], len(tiles_of(ITEMS[i - RING])) - 1)
                        act.wait_ge(full[bank_of(before)], e.use(full, before))
                    A(w_hi[:, i % RING, 0:n], raw[:, i % RING, 0:n], ACT.Copy).then_inc(w_hi_ready, 1)

                def rsqrt_of(key, width):
                    act.wait_ge(full[bank_of(key)], e.use(full, key))
                    src = bank[bank_of(key)]
                    A(rstd[:], src[:], ACT.Ln, scale=1.0 / width, bias=eps).then_inc(free[bank_of(key)], 1)
                    act.wait_ge(free[bank_of(key)], e.use(free, key))
                    A(rstd[:], rstd[:], ACT.Exp, scale=-0.5).then_inc(rstd_ready, 1)

                def gate_head(it):
                    act.wait_ge(full[bank_of((it, 0))], e.use(full, (it, 0)))
                    src = bank[bank_of((it, 0))]
                    if gated and gated[-1][0] in MERGES:
                        act.wait_ge(sigma_ready, e.at(sigma_ready, sum(g[0] in MERGES for g in gated)))
                    if silu_before:
                        before = (silu_before.pop(), 0)
                        act.wait_ge(free[bank_of(before)], e.use(free, before))
                    if it[0] in MERGES:
                        A(gate_t[:], src[:], ACT.Exp, scale=-1.0).then_inc(free[bank_of((it, 0))], 1)
                    else:
                        A(gate_t[:], src[:], ACT.Exp, scale=-1.0).then_inc(gate_exp, 1)
                    gated.append(it)

                def gate_tail(it):
                    act.wait_ge(gate_cap, e.at(gate_cap, len(gated)))
                    A(gate_t[:], gate_t[:], ACT.Ln, bias=one).then_inc(act_link, 1)
                    act.wait_ge(act_link, e.made(act_link))
                    if it[0] in MERGES:
                        mixer, j = "abc".index(it[0][1]), it[1]
                        if j >= 3:
                            act.wait_ge(free[bank_of((("p" + it[0][1], (j - 3) // 2), (j - 3) % 2))], e.use(free, (("p" + it[0][1], (j - 3) // 2), (j - 3) % 2)))
                        elif mixer:
                            act.wait_ge(free[bank_of((("p" + "abc"[mixer - 1], DT // 2 - 1), 1))], e.use(free, (("p" + "abc"[mixer - 1], DT // 2 - 1), 1)))
                        A(sigma[:, j % 3, :], gate_t[:], ACT.Exp, scale=-1.0).then_inc(sigma_ready, 1)
                    else:
                        A(gate_t[:], gate_t[:], ACT.Exp, scale=-1.0).then_inc(gate_sig, 1)
                        silu_before.append(it)

                def copy_out(key, dst, src=None):
                    act.wait_ge(full[bank_of(key)], e.use(full, key))
                    src = bank[bank_of(key)] if src is None else src
                    A(dst, src[:], ACT.Copy).then_inc(free[bank_of(key)], 1)

                def item(it):
                    i = ITEM_AT[it]
                    kind, j = it
                    if kind in ("q", "g", "bg", "cg", "ma", "mb", "mc"):
                        gate_head(it)
                        split(i + 2)
                        gate_tail(it)
                        return
                    if kind == "f":
                        act.wait_ge(full[bank_of((it, 0))], e.use(full, (it, 0)))
                        src = bank[bank_of((it, 0))]
                        A(hz_a[:], src[:], ACT.Abs).then_inc(act_link, 1)
                        act.wait_ge(act_link, e.made(act_link))
                        A(hz_a[:], hz_a[:], ACT.Exp, scale=-1.0).then_inc(act_link, 1)
                        act.wait_ge(act_link, e.made(act_link))
                        A(hz_a[:], hz_a[:], ACT.Ln, bias=one).then_inc(hz_ln, 1)
                        split(i + 2)
                        act.wait_ge(free[bank_of((it, 0))], e.use(free, (it, 0)))
                        A(hz_b[:], hz_b[:], ACT.Exp)
                        A(hz_c[:], hz_c[:], ACT.Exp).then_inc(hz_s, 1)
                        act.wait_ge(hz_f, e.at(hz_f, j + 1))
                        A(hz_c[:], hz_c[:], ACT.Ln)
                        A(hz_b[:], hz_b[:], ACT.Ln, scale=1.0 / TAU).then_inc(hz_l, 1)
                        return
                    split(i + 2)
                    if kind == "i":
                        copy_out((it, 0), hg_vt[:])
                        if j >= 2:
                            act.wait_ge(full[bank_of(("hg_pv", j - 2))], e.use(full, ("hg_pv", j - 2)))
                        copy_out(("hg_v", j), hg_v[:, j % 2, :, :].rearrange("p a b -> p (a b)"))
                    elif kind in ("cq", "ckv"):
                        n = j if kind == "cq" else CQT + j
                        act.wait_ge(full[bank_of((it, 0))], e.use(full, (it, 0)))
                        src = bank[bank_of((it, 0))]
                        if n >= 1:
                            act.wait_ge(cq_sum, e.at(cq_sum, n))
                        A(sq_t[:], src[:], ACT.Square).then_inc(cq_sq, 1)
                        copy_out((it, 0), cq_raw[:, j, :] if kind == "cq" else ckv_raw[:, j, :], src)
                    elif kind == "kr":
                        act.wait_ge(full[bank_of((it, 0))], e.use(full, (it, 0)))
                        src = bank[bank_of((it, 0))]
                        copy_out((it, 0), k_rope[0:96, :], src[0:96, :])
                    elif kind == "mla":
                        act.wait_ge(full[bank_of((it, 0))], e.use(full, (it, 0)))
                        src = bank[bank_of((it, 0))]
                        if j >= 2:
                            act.wait_ge(full[bank_of(("mla_s", j - 2, 2))], e.use(full, ("mla_s", j - 2, 2)))
                            act.wait_ge(full[bank_of(("mla_s", j - 2, 3))], e.use(full, ("mla_s", j - 2, 3)))
                        copy_out((it, 0), mla_q[0:96, j % 2, :], src[0:96, :])
                        copy_out((it, 1), mla_kv[:, j % 2, :])
                    elif kind in ("rq", "rk"):
                        act.wait_ge(full[bank_of((it, 0))], e.use(full, (it, 0)))
                        src = bank[bank_of((it, 0))]
                        if kind == "rq" and j == 0:
                            act.dma_start(ret_decay[:], decay).then_inc(decay_in, 16)
                        copy_out((it, 0), (ret_q if kind == "rq" else ret_k)[:, j, :], src)
                    elif kind == "rv":
                        copy_out((it, 0), ret_vt[:])
                    elif kind == "pc":
                        for m in (2 * j, 2 * j + 1):
                            act.wait_ge(mg_t, e.at(mg_t, m + 1))
                            A(mg_hi[:, m, :], merged[:, m, :], ACT.Copy).then_inc(mg_hi_ready, 1)
                    elif kind == "wo":
                        act.wait_ge(free[bank_of((it, 0))], e.use(free, (it, 0)))
                        if j >= 1:
                            act.wait_ge(x_sum, e.at(x_sum, j))
                        A(sq_t[:], x[:, j, :], ACT.Square).then_inc(x_sq, 1)

                for s in SCHEDULE:
                    kind = s[0]
                    if kind == "norm":
                        split(0)
                        split(1)
                        rsqrt_of(("ssq",), D_MODEL)
                        act.dma_start(cur[:], params_cur[layer]).then_inc(params_in, 16)
                        act.dma_start(nxt[:], params_nxt[layer]).then_inc(params_in, 16)
                        act.dma_start(mod_w[:, 0, :], w_mod[layer, 0]).then_inc(mod_in[0], 16)
                        for j in range(DT):
                            act.wait_ge(norm_t, e.at(norm_t, j + 1))
                            A(h_hi[:, j, :], (t1, t2)[j % 2][:], ACT.Identity, bias=shift[:, j:j + 1]).then_inc(norm_hi, 1)
                        act.wait_ge(lb_d_ready, e.at(lb_d_ready, 1))
                        A(lb_e[:], lb_e[:], ACT.Exp).then_inc(lb_e_ready, 1)
                    elif kind == "item":
                        item(s[1:])
                    elif kind == "hg_lv":
                        h, n = s[1:]
                        if n <= 6:
                            act.wait_ge(d_ready, e.at(d_ready, 7 * h + n + 1))
                        if n < 5:
                            A(hg_e[:, n % 2, :], hg_e[:, n % 2, :], ACT.Exp).then_inc(e_ready, 1)
                        elif n == 5:
                            act.wait_ge(x_built, e.at(x_built, 7 * h + 5))
                            A(hg_e[:, 0, :], hg_e[:, 1, :], ACT.Exp, scale=-1.0).then_inc(act_link, 1)
                            act.wait_ge(act_link, e.made(act_link))
                            A(hg_e[:, 1, :], hg_e[:, 1, :], ACT.Exp).then_inc(e_ready, 1)
                        elif n == 6:
                            b = hg_b[:, h % 2, :]
                            A(hg_e[:, 0, 0:3 * P], hg_e[:, 0, 0:3 * P], ACT.Exp)
                            A(g_last[:], b.rearrange("p (c t) -> p c t", t=P)[:, :, P - 1], ACT.Exp)
                            A(hg_e[:, 1, 0:3 * P], b[:, P:], ACT.Exp).then_inc(e_ready, 1)
                        else:
                            if h >= 1:
                                act.wait_ge(full[bank_of(("hg_pv", h - 1))], e.use(full, ("hg_pv", h - 1)))
                            act.wait_ge(full[bank_of(("cross0", h))], e.use(full, ("cross0", h)))
                            src = bank[bank_of(("cross0", h))]
                            A(hg_at[:, 0, P:], src[:, 0:3 * P], ACT.Copy)
                            copy_out(("cross0", h), hg_at[:, 2, 3 * P:], src[:, 3 * P:])
                            act.wait_ge(full[bank_of(("cross1", h))], e.use(full, ("cross1", h)))
                            src = bank[bank_of(("cross1", h))]
                            copy_out(("cross1", h), hg_at[:, 1, 2 * P:], src[:, 0:2 * P])
                    elif kind in ("hg_pv", "ret_pv"):
                        act.wait_ge(full[bank_of(s)], e.use(full, s))
                        src = bank[bank_of(s)]
                        A(o_sq[:], src[:], ACT.Square).then_inc(o_sq_ready, 1)
                    elif kind in ("hg_out", "ret_out"):
                        rsqrt_of(s, HG_DK if kind == "hg_out" else RET_DV)
                        n = s[1] + (0 if kind == "hg_out" else 2 * CH)
                        act.wait_ge(y_t_ready, e.at(y_t_ready, n + 1))
                        A((y_hi if kind == "hg_out" else yc_hi)[:, s[1], :], y_t[:], ACT.Copy).then_inc(y_hi_ready, 1)
                    elif kind in ("cq_norm", "ckv_norm"):
                        rsqrt_of(s, D_CQ if kind == "cq_norm" else D_C)
                        raws, his, n0, n = (cq_raw, cq_hi, 0, CQT) if kind == "cq_norm" else (ckv_raw, ckv_hi, CQT, CKT)
                        for j in range(n):
                            act.wait_ge(cqn_t, e.at(cqn_t, n0 + j + 1))
                            A(his[:, j, :], raws[:, j, :], ACT.Copy).then_inc(cqn_hi, 1)
                    elif kind == "ret_v":
                        copy_out(s, ret_v[:, s[1], :, :].rearrange("p a b -> p (a b)"))
                    elif kind == "mla_qk":
                        h = s[1]
                        act.wait_ge(full[bank_of(("mla_v", h))], e.use(full, ("mla_v", h)))
                        src = bank[bank_of(("mla_v", h))]
                        if h >= 4:
                            act.wait_ge(full[bank_of(("mla_pv", h - 4))], e.use(full, ("mla_pv", h - 4)))
                        a = 0 if h % 2 == 0 else 2 * MLA_DV
                        copy_out(("mla_v", h), v_ones[:, (h // 2) % 2, :, a:a + MLA_DV],
                                 src[:].rearrange("p (a b) -> p a b", b=P)[:, :, NOPE:])
                    elif kind == "mla_s":
                        h, qi = s[1:]
                        n = CH * h + qi
                        if n >= 2:
                            act.wait_ge(full[bank_of(("mla_t", (n - 2) // CH, (n - 2) % CH))], e.use(full, ("mla_t", (n - 2) // CH, (n - 2) % CH)))
                        act.wait_ge(p_max, e.at(p_max, n + 1))
                        src = bank[USES[s][0]]
                        w = (qi + 1) * P
                        A(mla_p[:, qi % 2, 0:w], src[:, 0:w], ACT.Exp, scale=MLA_SCALE, bias=neg_max[:, qi:qi + 1]).then_inc(free[bank_of(s)], 1)
                    elif kind == "mla_t" and s[2] % 2 == 0:
                        h, qi = s[1:]
                        act.wait_ge(full[bank_of(s)], e.use(full, s))
                        src = bank[bank_of(s)]
                        if h >= 1:
                            act.wait_ge(full[bank_of(("mla_pv", h - 1))], e.use(full, ("mla_pv", h - 1)))
                        copy_out(s, mla_pt[:, 0:qi + 1, qi * P:(qi + 1) * P],
                                 src[:, 0:(qi + 1) * P].rearrange("p (a b) -> p a b", b=P))
                    elif kind == "mla_pv":
                        h = s[1]
                        own, other = (slice(0, MLA_DV), slice(MLA_DV, P))[::1 if h % 2 == 0 else -1]
                        act.wait_ge(full[bank_of(s)], e.use(full, s))
                        src = bank[bank_of(s)]
                        A(rstd[own, :], src[other, :], ACT.Ln).then_inc(act_link, 1)
                        act.wait_ge(act_link, e.made(act_link))
                        A(rstd[own, :], rstd[own, :], ACT.Exp, scale=-1.0).then_inc(rstd_ready, 1)
                        if h % 2 == 1:
                            pair = h // 2
                            if pair == 0:
                                act.wait_ge(full[bank_of((("pa", DT // 2 - 1), 1))], e.use(full, (("pa", DT // 2 - 1), 1)))
                            act.wait_ge(y_t_ready, e.at(y_t_ready, CH + pair + 1))
                            A(y_hi[:, pair, :], y_t[:], ACT.Copy).then_inc(y_hi_ready, 1)
                    elif kind == "mod_acc":
                        n = DT * s[1] + s[2] + 1
                        if n < MOD_SECTIONS * DT:
                            if n >= 2:
                                act.wait_ge(mod_done, e.at(mod_done, n - 1))
                            act.dma_start(mod_w[:, n % 2, :], w_mod[layer, n]).then_inc(mod_in[n % 2], 16)
            assert e.own[id(act_link)] == PER_LAYER["act_link"], e.own[id(act_link)]
            act.wait_ge(fin_sum, 1)
            A(rstd[:], bank["misc"][:], ACT.Ln, scale=1.0 / D_MODEL, bias=eps).then_inc(fin_link, 1)
            act.wait_ge(fin_link, 1)
            A(rstd[:], rstd[:], ACT.Exp, scale=-0.5).then_inc(fin_rstd, 1)

        @block.vector
        def _(dve):
            V = nc.vector
            links = [0]

            def link(ins):
                links[0] += 1
                ins.then_inc(pro_link, 1)
                dve.wait_ge(pro_link, links[0])

            link(V.memset(v_ones[:], 1.0))
            dve.wait_ge(const_in, 16)
            link(V.tensor_copy(ident_bf[:], ident))
            link(V.tensor_copy(neg_bf[:], c("neg")))
            dve.wait_ge(cond_e, 1)
            link(V.tensor_scalar(cond_t[:], cond_t[:], EXP_CAP, 1.0, ALU.min, ALU.add))
            link(V.reciprocal(cond_t[:], cond_t[:]))
            link(V.tensor_tensor(cond[:], cond_t[:], c("c"), ALU.mult))
            dve.wait_ge(pos_in, 16)
            link(V.tensor_copy(pos_f[:], pos_i[:]))
            n = 0
            for inv in ("inv_mla", "inv_ret"):
                link(V.tensor_scalar(ang[:], pos_f[:], c(inv), None, ALU.mult))
                for quarter in (0.0, 0.25):
                    link(V.tensor_scalar(turn[:], ang[:], 1.0 / (2.0 * np.pi), quarter, ALU.mult, ALU.add))
                    link(V.tensor_scalar(turn[:], turn[:], ROUND, -ROUND, ALU.add, ALU.add))
                    r = red[:, n, :]
                    link(V.scalar_tensor_tensor(r, turn[:], -TWO_PI[0], ang[:], ALU.mult, ALU.add))
                    link(V.scalar_tensor_tensor(r, turn[:], -TWO_PI[1], r, ALU.mult, ALU.add))
                    link(V.scalar_tensor_tensor(r, turn[:], -TWO_PI[2], r, ALU.mult, ALU.add))
                    link(V.tensor_scalar(r, r, quarter * 2.0 * np.pi, PI_BELOW, ALU.add, ALU.min))
                    V.tensor_scalar(r, r, -PI_BELOW, None, ALU.max).then_inc(angles, 1)
                    n += 1
            for n in range(2 * DT):
                sec, k = divmod(n, DT)
                acc = pro_acc[:, sec * D_MODEL:(sec + 1) * D_MODEL]
                dve.wait_ge(pro_in[n % PRO_RING], 16 * (n // PRO_RING + 1))
                if k == 0:
                    ins = V.tensor_scalar(acc, pro_w[:, n % PRO_RING, :], cond[:, k:k + 1], None, ALU.mult)
                else:
                    ins = V.scalar_tensor_tensor(acc, pro_w[:, n % PRO_RING, :], cond[:, k:k + 1], acc, ALU.mult, ALU.add)
                ins.then_inc(pro_mod_done, 1)
                dve.wait_ge(pro_mod_done, n + 1)
            for j in range(DT):
                dve.wait_ge(pro_sq, j + 1)
                src = (sq_t, o_sq)[j % 2][:]
                ins = V.tensor_copy(sq_sum[:], src) if j == 0 else V.tensor_tensor(sq_sum[:], sq_sum[:], src, ALU.add)
                ins.then_inc(pro_sum, 1)
                dve.wait_ge(pro_sum, j + 1)
            dve.wait_ge(par_in, 16)
            dve.wait_ge(pro_mod_sum, 1)
            link(V.tensor_tensor(shift[:], bank["misc"][:, 0:DT], pn("b_shift"), ALU.add))
            link(V.tensor_tensor(scale_g[:], bank["misc"][:, DT:2 * DT], pn("b_scale"), ALU.add))
            dve.wait_ge(tables, 4)
            V.scalar_tensor_tensor(scale_g[:], scale_g[:], 1.0, pn("norm_g"), ALU.add, ALU.mult).then_inc(sq_sum_ready, 1)

            with dve.Fori(0, DEPTH) as layer:
                e = Counter(dve, layer, per_layer)
                dve.wait_ge(sq_sum_ready, layer + 1)
                gated = []

                def lo_part(dst, full_value, hi, sig):
                    V.tensor_tensor(dst, full_value, hi.bitcast(F32), ALU.subtract).then_inc(sig, 1)

                def rope(key, src, cos, sin, dst, sig):
                    r, swapped = src
                    dve.wait_ge(full[bank_of(key)], e.use(full, key))
                    ps = bank[bank_of(key)]
                    V.tensor_tensor(t1[swapped, :], r, cos[swapped, :], ALU.mult).then_inc(dve_link, 1)
                    dve.wait_ge(dve_link, e.made(dve_link))
                    V.tensor_tensor(t2[swapped, :], ps[swapped, :], sin[swapped, :], ALU.mult).then_inc(free[bank_of(key)], 1)
                    dve.wait_ge(free[bank_of(key)], e.use(free, key))
                    V.tensor_tensor(dst, t1[swapped, :], t2[swapped, :], ALU.add).then_inc(sig, 1)
                    dve.wait_ge(sig, e.made(sig))

                def cap(it):
                    gated.append(it)
                    if it[0] in MERGES:
                        dve.wait_ge(free[bank_of((it, 0))], e.use(free, (it, 0)))
                    else:
                        dve.wait_ge(gate_exp, e.at(gate_exp, sum(g[0] not in MERGES for g in gated)))
                    V.tensor_scalar(gate_t[:], gate_t[:], EXP_CAP, None, ALU.min).then_inc(gate_cap, 1)

                def silu(it, dst, factor=None):
                    cap(it)
                    dve.wait_ge(gate_sig, e.at(gate_sig, sum(g[0] not in MERGES for g in gated)))
                    ps = bank[USES[(it, 0)][0]]
                    if factor is None:
                        V.tensor_tensor(dst, ps[:], gate_t[:], ALU.mult).then_inc(free[bank_of((it, 0))], 1)
                        dve.wait_ge(free[bank_of((it, 0))], e.use(free, (it, 0)))
                    else:
                        V.scalar_tensor_tensor(dst, ps[:], factor, gate_t[:], ALU.mult, ALU.mult).then_inc(free[bank_of((it, 0))], 1)
                        dve.wait_ge(free[bank_of((it, 0))], e.use(free, (it, 0)))

                def item(it):
                    kind, j = it
                    if kind == "f":
                        dve.wait_ge(hz_ln, e.at(hz_ln, j + 1))
                        ps = bank[USES[(it, 0)][0]]
                        V.scalar_tensor_tensor(hz_b[:], ps[:], 0.0, hz_a[:], ALU.min, ALU.subtract).then_inc(dve_link, 1)
                        dve.wait_ge(dve_link, e.made(dve_link))
                        V.tensor_tensor(hz_c[:], hz_b[:], ps[:], ALU.subtract).then_inc(free[bank_of((it, 0))], 1)
                        dve.wait_ge(free[bank_of((it, 0))], e.use(free, (it, 0)))
                        dve.wait_ge(hz_s, e.at(hz_s, j + 1))
                        V.tensor_scalar(hz_b[:], hz_b[:], one_lb[:, j:j + 1], lb[:, j:j + 1], ALU.mult, ALU.add).then_inc(dve_link, 1)
                        dve.wait_ge(dve_link, e.made(dve_link))
                        V.tensor_scalar(hg_k[:, j % 2, :], hz_c[:], one_lb[:, j:j + 1], None, ALU.mult).then_inc(dve_link, 1)
                        dve.wait_ge(dve_link, e.made(dve_link))
                        V.tensor_scalar(hz_c[:], hz_b[:], TAU, None, ALU.max).then_inc(dve_link, 1)
                        dve.wait_ge(dve_link, e.made(dve_link))
                        V.tensor_scalar(hz_b[:], hz_b[:], LOG_FLOOR, TAU, ALU.max, ALU.min).then_inc(hz_f, 1)
                        dve.wait_ge(hz_f, e.made(hz_f))
                        dve.wait_ge(hz_l, e.at(hz_l, j + 1))
                        V.tensor_tensor(hz_b[:], hz_b[:], hz_c[:], ALU.add).then_inc(dve_link, 1)
                        dve.wait_ge(dve_link, e.made(dve_link))
                        V.tensor_tensor_scan(hg_b[:, j % 2, :], c("reset"), hz_b[:], 0.0, ALU.mult, ALU.add).then_inc(b_ready, 1)
                        dve.wait_ge(b_ready, e.made(b_ready))
                    elif kind == "q":
                        silu(it, hg_q[:, j % 2, :], HG_DK ** -0.5)
                    elif kind == "g":
                        silu(it, hg_g[:, j % 2, :])
                    elif kind == "bg":
                        silu(it, mla_g[:, j % 2, :])
                    elif kind == "cg":
                        silu(it, ret_g[:])
                    elif kind in MERGES:
                        cap(it)
                    elif kind in ("cq", "ckv"):
                        n = j if kind == "cq" else CQT + j
                        dve.wait_ge(cq_sq, e.at(cq_sq, n + 1))
                        if j == 0:
                            V.tensor_copy(sq_sum[:], sq_t[:]).then_inc(cq_sum, 1)
                            dve.wait_ge(cq_sum, e.made(cq_sum))
                        else:
                            V.tensor_tensor(sq_sum[:], sq_sum[:], sq_t[:], ALU.add).then_inc(cq_sum, 1)
                            dve.wait_ge(cq_sum, e.made(cq_sum))
                    elif kind in ("pa", "pb", "pc"):
                        mixer = "abc".index(kind[1])
                        for t in range(2):
                            m = 2 * j + t
                            dve.wait_ge(full[bank_of((it, t))], e.use(full, (it, t)))
                            ps = bank[bank_of((it, t))]
                            dve.wait_ge(sigma_ready, e.at(sigma_ready, mixer * DT + m + 1))
                            dst = merged[:, m, :] if mixer == 0 else t1[:]
                            V.tensor_tensor(dst, ps[:], sigma[:, m % 3, :], ALU.mult).then_inc(free[bank_of((it, t))], 1)
                            dve.wait_ge(free[bank_of((it, t))], e.use(free, (it, t)))
                            if mixer == 1:
                                V.tensor_tensor(merged[:, m, :], merged[:, m, :], t1[:], ALU.add).then_inc(dve_link, 1)
                                dve.wait_ge(dve_link, e.made(dve_link))
                            elif mixer == 2:
                                V.tensor_tensor(merged[:, m, :], merged[:, m, :], t1[:], ALU.add).then_inc(mg_t, 1)
                                dve.wait_ge(mg_t, e.made(mg_t))
                        if mixer == 2:
                            for m in (2 * j, 2 * j + 1):
                                dve.wait_ge(mg_hi_ready, e.at(mg_hi_ready, m + 1))
                                lo_part(mg_lo[:, m, :], merged[:, m, :], mg_hi[:, m, :], mg_ready)
                    elif kind == "wo":
                        dve.wait_ge(full[bank_of((it, 0))], e.use(full, (it, 0)))
                        ps = bank[bank_of((it, 0))]
                        V.scalar_tensor_tensor(x[:, j, :], ps[:], gate[:, j:j + 1], x[:, j, :], ALU.mult, ALU.add).then_inc(free[bank_of((it, 0))], 1)
                        dve.wait_ge(free[bank_of((it, 0))], e.use(free, (it, 0)))
                        if j >= 1:
                            add_square(j - 1)

                def add_square(j):
                    dve.wait_ge(x_sq, e.at(x_sq, j + 1))
                    ins = V.tensor_copy(sq_sum[:], sq_t[:]) if j == 0 else V.tensor_tensor(sq_sum[:], sq_sum[:], sq_t[:], ALU.add)
                    if j < DT - 1:
                        ins.then_inc(x_sum, 1)
                        dve.wait_ge(x_sum, e.made(x_sum))
                    else:
                        ins.then_inc(sq_sum_ready, 1)

                def level_exponents(h, n):
                    b = hg_b[:, h % 2, :]
                    if n < 5:
                        half = LEVELS[n]
                        bv = b.rearrange("p (c s m) -> p c s m", s=2, m=half)
                        ev = hg_e[:, n % 2, :].rearrange("p (c s m) -> p c s m", s=2, m=half)
                        nb = SEQ // (2 * half)
                        ref = bv[:, :, 0, half - 1:half].to_broadcast([P, nb, half])
                        V.tensor_tensor(ev[:, :, 0, :], ref, bv[:, :, 0, :], ALU.subtract)
                        V.tensor_tensor(ev[:, :, 1, :], bv[:, :, 1, :], ref, ALU.subtract).then_inc(d_ready, 1)
                        dve.wait_ge(d_ready, e.made(d_ready))
                    elif n == 5:
                        bv = b.rearrange("p (c m) -> p c m", m=BASE)
                        V.tensor_tensor(centre[:], bv[:, :, 1], bv[:, :, 2], ALU.add).then_inc(dve_link, 1)
                        dve.wait_ge(dve_link, e.made(dve_link))
                        V.scalar_tensor_tensor(hg_e[:, 1, :].rearrange("p (c m) -> p c m", m=BASE),
                                               centre[:, :, None].to_broadcast([P, SEQ // BASE, BASE]), -0.5, bv,
                                               ALU.mult, ALU.add).then_inc(d_ready, 1)
                        dve.wait_ge(d_ready, e.made(d_ready))
                    else:
                        bv = b.rearrange("p (c m) -> p c m", m=P)[:, 0:3, :]
                        V.tensor_tensor(hg_e[:, 0, 0:3 * P].rearrange("p (c m) -> p c m", m=P),
                                        bv[:, :, P - 1:P].to_broadcast([P, 3, P]), bv, ALU.subtract).then_inc(d_ready, 1)
                        dve.wait_ge(d_ready, e.made(d_ready))

                def level_operands(h, n):
                    q, k = hg_q[:, h % 2, :], hg_k[:, h % 2, :]
                    dve.wait_ge(e_ready, e.at(e_ready, 7 * h + n + 1))
                    if 2 <= n < 5:
                        dve.wait_ge(full[bank_of(("lv", h, n - 2))], e.use(full, ("lv", h, n - 2)))
                    elif n == 5:
                        dve.wait_ge(full[bank_of(("lv", h, 3))], e.use(full, ("lv", h, 3)))
                        dve.wait_ge(full[bank_of(("lv", h, 4))], e.use(full, ("lv", h, 4)))
                    elif n < 2 and h:
                        dve.wait_ge(full[bank_of(("lv", h - 1, 5))], e.use(full, ("lv", h - 1, 5)))
                    elif n == 6 and h:
                        dve.wait_ge(full[bank_of(("cross0", h - 1))], e.use(full, ("cross0", h - 1)))
                        dve.wait_ge(full[bank_of(("cross1", h - 1))], e.use(full, ("cross1", h - 1)))
                    if n < 5:
                        def v(t):
                            return t.rearrange("p (c s m) -> p c s m", s=2, m=LEVELS[n])
                        V.tensor_tensor(v(hg_x[:, n % 2, :])[:, :, 0, :], v(hg_e[:, n % 2, :])[:, :, 0, :],
                                        v(k)[:, :, 0, :], ALU.mult)
                        V.tensor_tensor(v(hg_x[:, n % 2, :])[:, :, 1, :], v(hg_e[:, n % 2, :])[:, :, 1, :],
                                        v(q)[:, :, 1, :], ALU.mult).then_inc(x_built, 1)
                        dve.wait_ge(x_built, e.made(x_built))
                    elif n == 5:
                        V.tensor_tensor(hg_x[:, 0, :], hg_e[:, 0, :], k, ALU.mult)
                        V.tensor_tensor(hg_x[:, 1, :], hg_e[:, 1, :], q, ALU.mult).then_inc(x_built, 1)
                        dve.wait_ge(x_built, e.made(x_built))
                    else:
                        def v(t):
                            return t.rearrange("p (c m) -> p c m", m=P)
                        V.tensor_tensor(hg_qc[:, :, 0:P], v(q[:, P:]), v(hg_e[:, 1, 0:3 * P]), ALU.mult).then_inc(dve_link, 1)
                        dve.wait_ge(dve_link, e.made(dve_link))
                        V.tensor_scalar(hg_qc[:, 1, P:2 * P], hg_qc[:, 2, 0:P], g_last[:, 2:3], None, ALU.mult).then_inc(dve_link, 1)
                        dve.wait_ge(dve_link, e.made(dve_link))
                        V.tensor_scalar(hg_qc[:, 0, P:3 * P], hg_qc[:, 1, 0:2 * P], g_last[:, 1:2], None, ALU.mult).then_inc(dve_link, 1)
                        dve.wait_ge(dve_link, e.made(dve_link))
                        V.tensor_tensor(hg_kd[:], hg_e[:, 0, 0:3 * P], k[:, 0:3 * P], ALU.mult).then_inc(x_built, 1)
                        dve.wait_ge(x_built, e.made(x_built))

                def level_select(h, n):
                    dve.wait_ge(full[bank_of(("lv", h, n))], e.use(full, ("lv", h, n)))
                    ps = bank[bank_of(("lv", h, n))]
                    src = ps[:].rearrange("p (c t) -> p c t", t=P)
                    mask = c(("m64", "m32", "m16", "m8", "m4", "mbase")[n])
                    if n == 0:
                        if h:
                            dve.wait_ge(full[bank_of(("hg_pv", h - 1))], e.use(full, ("hg_pv", h - 1)))
                        ins = V.tensor_tensor(diagonal(hg_at), src, mask[:, None, :].to_broadcast([P, CH, P]), ALU.mult)
                    else:
                        V.tensor_copy(carry[:], one)
                        ins = V.copy_predicated(diagonal(hg_at), mask.bitcast(U32)[:, None, :].to_broadcast([P, CH, P]), src)
                    ins.then_inc(free[bank_of(("lv", h, n))], 1)
                    dve.wait_ge(free[bank_of(("lv", h, n))], e.use(free, ("lv", h, n)))

                def y_out(n, hi, lo):
                    dve.wait_ge(y_hi_ready, e.at(y_hi_ready, n + 1))
                    lo_part(lo, y_t[:], hi, y_ready)

                rstd_uses = [0]

                def next_rstd():
                    rstd_uses[0] += 1
                    dve.wait_ge(rstd_ready, e.at(rstd_ready, rstd_uses[0]))

                for s in SCHEDULE:
                    kind = s[0]
                    if kind == "norm":
                        next_rstd()
                        for j in range(DT + 1):
                            if j < DT:
                                V.scalar_tensor_tensor((t1, t2)[j % 2][:], x[:, j, :], scale_g[:, j:j + 1], rstd[:],
                                                       ALU.mult, ALU.mult).then_inc(norm_t, 1)
                                dve.wait_ge(norm_t, e.made(norm_t))
                            if j >= 1:
                                i = j - 1
                                dve.wait_ge(norm_hi, e.at(norm_hi, i + 1))
                                V.scalar_tensor_tensor(h_lo[:, i, :], (t1, t2)[i % 2][:], shift[:, i:i + 1],
                                                       h_hi[:, i, :].bitcast(F32), ALU.add, ALU.subtract).then_inc(h_ready, 1)
                                dve.wait_ge(h_ready, e.made(h_ready))
                        dve.wait_ge(params_in, e.at(params_in, 32))
                        lg = pc("logits").rearrange("p (l h) -> p l h", h=HG_HEADS)
                        V.tensor_tensor(lb_t[:], lg[:, 0, :], lg[:, 1, :], ALU.max).then_inc(dve_link, 1)
                        dve.wait_ge(dve_link, e.made(dve_link))
                        for i in range(2, DEPTH):
                            V.tensor_tensor(lb_t[:], lb_t[:], lg[:, i, :], ALU.max).then_inc(dve_link, 1)
                            dve.wait_ge(dve_link, e.made(dve_link))
                        V.tensor_tensor(lb_e[:], lg, lb_t[:, None, :].to_broadcast([P, DEPTH, HG_HEADS]), ALU.subtract).then_inc(lb_d_ready, 1)
                        dve.wait_ge(lb_d_ready, e.made(lb_d_ready))
                        dve.wait_ge(lb_e_ready, e.at(lb_e_ready, 1))
                        V.tensor_tensor(lb_t[:], lb_e[:, 0, :], lb_e[:, 1, :], ALU.add).then_inc(dve_link, 1)
                        dve.wait_ge(dve_link, e.made(dve_link))
                        for i in range(2, DEPTH):
                            V.tensor_tensor(lb_t[:], lb_t[:], lb_e[:, i, :], ALU.add).then_inc(dve_link, 1)
                            dve.wait_ge(dve_link, e.made(dve_link))
                        V.reciprocal(lb_t[:], lb_t[:]).then_inc(dve_link, 1)
                        dve.wait_ge(dve_link, e.made(dve_link))
                        V.tensor_scalar(lb[:], lb_e[:, 0, :], pc("sel")[:, 0:1], None, ALU.mult).then_inc(dve_link, 1)
                        dve.wait_ge(dve_link, e.made(dve_link))
                        for i in range(1, DEPTH):
                            V.scalar_tensor_tensor(lb[:], lb_e[:, i, :], pc("sel")[:, i:i + 1], lb[:], ALU.mult, ALU.add).then_inc(dve_link, 1)
                            dve.wait_ge(dve_link, e.made(dve_link))
                        V.tensor_tensor(lb[:], lb[:], lb_t[:], ALU.mult).then_inc(dve_link, 1)
                        dve.wait_ge(dve_link, e.made(dve_link))
                        V.tensor_scalar(one_lb[:], lb[:], -1.0, 1.0, ALU.mult, ALU.add).then_inc(dve_link, 1)
                        dve.wait_ge(dve_link, e.made(dve_link))
                    elif kind == "item":
                        item(s[1:])
                    elif kind == "hg_lv":
                        h, n = s[1:]
                        if n < 6:
                            level_exponents(h, n)
                        if n >= 1:
                            level_operands(h, n - 1)
                        if n == 6:
                            level_exponents(h, n)
                        if n >= 2:
                            level_select(h, n - 2)
                    elif kind in ("hg_out", "ret_out"):
                        next_rstd()
                        h = s[1]
                        key = (kind.replace("out", "pv"), h)
                        ps = bank["o"]
                        if kind == "hg_out":
                            ins = V.scalar_tensor_tensor(y_t[:], ps[:], pc("onorm"), rstd[:], ALU.mult, ALU.mult)
                        else:
                            ins = V.tensor_tensor(y_t[:], ps[:], rstd[:], ALU.mult)
                        ins.then_inc(free[bank_of(key)], 1)
                        dve.wait_ge(free[bank_of(key)], e.use(free, key))
                        V.tensor_tensor(y_t[:], y_t[:], hg_g[:, h % 2, :] if kind == "hg_out" else ret_g[:], ALU.mult).then_inc(y_t_ready, 1)
                        dve.wait_ge(y_t_ready, e.made(y_t_ready))
                        if kind == "hg_out":
                            y_out(h, y_hi[:, h, :], y_lo[:, h, :])
                        else:
                            y_out(2 * CH + h, yc_hi[:, h, :], yc_lo[:, h, :])
                    elif kind in ("cq_norm", "ckv_norm"):
                        next_rstd()
                        g, raws, his, los, n0, n = ((pc("g_cq"), cq_raw, cq_hi, cq_lo, 0, CQT) if kind == "cq_norm" else
                                                    (pc("g_ckv"), ckv_raw, ckv_hi, ckv_lo, CQT, CKT))
                        for j in range(n + 1):
                            if j < n:
                                V.scalar_tensor_tensor(raws[:, j, :], raws[:, j, :], g[:, j:j + 1], rstd[:],
                                                       ALU.mult, ALU.mult).then_inc(cqn_t, 1)
                                dve.wait_ge(cqn_t, e.made(cqn_t))
                            if j >= 1:
                                dve.wait_ge(cqn_hi, e.at(cqn_hi, n0 + j))
                                lo_part(los[:, j - 1, :], raws[:, j - 1, :], his[:, j - 1, :], cqn_ready)
                    elif kind == "kr_rope":
                        r = slice(NOPE, NOPE + ROPE)
                        rope(s, (k_rope[r, :], r), cos_mla, sin_mla, k_rope[r, :], dve_link)
                    elif kind == "ret_rope":
                        t = (ret_q if s[1] == "rq" else ret_k)[:, s[2], :]
                        rope(s, (t, slice(0, P)), cos_ret, sin_ret, t, ret_qk_ready)
                    elif kind == "mla_qk":
                        h = s[1]
                        r = slice(NOPE, NOPE + ROPE)
                        rope(("mla_swap", h), (mla_q[r, h % 2, :], r), cos_mla, sin_mla, mla_q[r, h % 2, :], q_ready)
                        dve.wait_ge(full[bank_of(("mla_v", h))], e.use(full, ("mla_v", h)))
                        V.tensor_copy(mla_kv[r, h % 2, :], k_rope[r, :]).then_inc(k_ready, 1)
                        dve.wait_ge(k_ready, e.made(k_ready))
                    elif kind == "mla_s":
                        h, qi = s[1:]
                        dve.wait_ge(full[bank_of(s)], e.use(full, s))
                        ps = bank[bank_of(s)]
                        V.reduce_max(row_max[:, qi:qi + 1], ps[:, 0:(qi + 1) * P], axis=AX.X).then_inc(dve_link, 1)
                        dve.wait_ge(dve_link, e.made(dve_link))
                        V.tensor_scalar(neg_max[:, qi:qi + 1], row_max[:, qi:qi + 1], -MLA_SCALE, None, ALU.mult).then_inc(p_max, 1)
                        dve.wait_ge(p_max, e.made(p_max))
                    elif kind == "mla_t" and s[2] % 2 == 1:
                        h, qi = s[1:]
                        dve.wait_ge(full[bank_of(s)], e.use(full, s))
                        ps = bank[bank_of(s)]
                        if h >= 1:
                            dve.wait_ge(full[bank_of(("mla_pv", h - 1))], e.use(full, ("mla_pv", h - 1)))
                        V.tensor_copy(mla_pt[:, 0:qi + 1, qi * P:(qi + 1) * P],
                                      ps[:, 0:(qi + 1) * P].rearrange("p (a b) -> p a b", b=P)).then_inc(free[bank_of(s)], 1)
                        dve.wait_ge(free[bank_of(s)], e.use(free, s))
                    elif kind == "mla_pv":
                        h = s[1]
                        own = slice(0, MLA_DV) if h % 2 == 0 else slice(MLA_DV, P)
                        next_rstd()
                        V.tensor_tensor(y_t[own, :], bank["o"][own, :], rstd[own, :], ALU.mult).then_inc(free[bank_of(s)], 1)
                        dve.wait_ge(free[bank_of(s)], e.use(free, s))
                        if h % 2 == 1:
                            V.tensor_tensor(y_t[:], y_t[:], mla_g[:, (h // 2) % 2, :], ALU.mult).then_inc(y_t_ready, 1)
                            dve.wait_ge(y_t_ready, e.made(y_t_ready))
                            y_out(CH + h // 2, y_hi[:, h // 2, :], y_lo[:, h // 2, :])
                    elif kind == "ret_s":
                        h, k = s[1:]
                        dve.wait_ge(full[bank_of(s)], e.use(full, s))
                        ps = bank[bank_of(s)]
                        if e.new(decay_in, 16):
                            dve.wait_ge(decay_in, e.at(decay_in, 16))
                        if h >= 1:
                            dve.wait_ge(full[bank_of(("ret_pv", h - 1))], e.use(full, ("ret_pv", h - 1)))
                        V.tensor_tensor(ret_sc[:, k, k * P:], ps[:, 0:SEQ - k * P], ret_decay[:, h, 0:SEQ - k * P],
                                        ALU.mult).then_inc(free[bank_of(s)], 1)
                        dve.wait_ge(free[bank_of(s)], e.use(free, s))
                    elif kind == "mod_acc":
                        sec, k = s[1:]
                        n = DT * sec + k
                        dve.wait_ge(mod_in[n % 2], e.at(mod_in[n % 2], 16 * (n // 2 + 1)))
                        if k == 0:
                            if sec:
                                dve.wait_ge(full[bank_of(("mod_sum", sec - 1))], e.use(full, ("mod_sum", sec - 1)))
                            ins = V.tensor_scalar(mod_acc[:], mod_w[:, n % 2, :], cond[:, k:k + 1], None, ALU.mult)
                        else:
                            ins = V.scalar_tensor_tensor(mod_acc[:], mod_w[:, n % 2, :], cond[:, k:k + 1], mod_acc[:],
                                                         ALU.mult, ALU.add)
                        ins.then_inc(mod_done, 1)
                        dve.wait_ge(mod_done, e.made(mod_done))
                    elif kind == "mod_sum":
                        what, part = divmod(s[1], MOD_SECTIONS // 3)
                        r = slice(part * (MOD_W // P), (part + 1) * (MOD_W // P))
                        dve.wait_ge(full[bank_of(s)], e.use(full, s))
                        ps = bank[bank_of(s)][:, 0:MOD_W // P]
                        dst, bias = ((gate, pc("b_gate")), (shift, pn("b_shift")), (scale_g, pn("b_scale")))[what]
                        V.tensor_tensor(dst[:, r], ps, bias[:, r], ALU.add).then_inc(free[bank_of(s)], 1)
                        dve.wait_ge(free[bank_of(s)], e.use(free, s))
                        if what == 2:
                            V.scalar_tensor_tensor(dst[:, r], dst[:, r], 1.0, pn("norm_g")[:, r], ALU.add, ALU.mult).then_inc(dve_link, 1)
                            dve.wait_ge(dve_link, e.made(dve_link))
                    elif kind == "end":
                        add_square(DT - 1)
            assert e.own[id(dve_link)] == PER_LAYER["dve_link"], e.own[id(dve_link)]
            dve.wait_ge(fin_rstd, 1)
            for j in range(DT):
                V.scalar_tensor_tensor(o_t[:, j, :], x[:, j, :], c("final_g")[:, j:j + 1], rstd[:], ALU.mult, ALU.mult)\
                    .then_inc(fin_out, 1)


def constants():
    cs = np.zeros((P, N_CST), np.float32)

    def put(name, a):
        cs[:, CST[name][0]:CST[name][1]] = a

    i = np.arange(P)
    put("ident", np.eye(P))
    put("ones", 1.0)
    for name, half, on in (("perm_mla", ROPE // 2, (i >= NOPE) & (i < NOPE + ROPE)), ("perm_ret", RET_DK // 2, i >= 0)):
        m = np.zeros((P, P))
        for d in i[on]:
            second = (d // half) % 2
            m[d - half if second else d + half, d] = 1.0 if second else -1.0
        put(name, m)
    for name, half in zip(("m64", "m32", "m16", "m8", "m4"), LEVELS):
        put(name, (i[:, None] // (2 * half) == i[None, :] // (2 * half)) & (i[:, None] % (2 * half) < half)
            & (i[None, :] % (2 * half) >= half))
    put("mbase", (i[:, None] // BASE == i[None, :] // BASE) & (i[:, None] <= i[None, :]))
    put("reset", np.arange(SEQ) % P != 0)
    put("neg", np.where(i[None, :] > i[:, None], -1e30, 0.0))
    for name, dim, lane in (("inv_mla", ROPE, i % (ROPE // 2)), ("inv_ret", RET_DK, i % (RET_DK // 2))):
        put(name, (np.float32(10000.0) ** (-(2 * lane).astype(np.float32) / np.float32(dim)))[:, None])
    put("eps", EPS)
    put("one", 1.0)
    log_gamma = np.log1p(-np.exp2(-5.0 - np.arange(RET_HEADS)))
    rel = np.arange(SEQ)[None, :] - i[:, None]
    decay = np.where(rel >= 0, np.exp(log_gamma[:, None, None] * np.maximum(rel, 0)), 0.0) * RET_DK ** -0.5
    return cs, decay.transpose(1, 0, 2).astype(np.float32)


def columns(v, tiles):
    return np.moveaxis(v.reshape(*v.shape[:-1], tiles, P), -1, -2)


def item_weights(item, l, a):
    kind, j = item
    w_in = a["w_in"][l]

    def cols(w, first, n):
        return w[:, first:first + n].reshape(-1, P, n).transpose(1, 0, 2)

    at = {"q": "a_q", "f": "a_f", "i": "a_i", "g": "a_g", "cq": "b_cq", "ckv": "b_ckv", "bg": "b_g", "rq": "c_q", "rk": "c_k",
          "rv": "c_v", "cg": "c_g", "ma": "m_a", "mb": "m_b", "mc": "m_c"}
    if kind in at:
        return cols(w_in, OFF[at[kind]] + P * j, P).reshape(P, -1)
    if kind == "kr":
        return np.tile(cols(w_in, OFF["b_kr"], ROPE), (1, 1, 3)).reshape(P, -1)
    if kind == "mla":
        uq = cols(a["mla_w_uq"][l], j * (NOPE + ROPE), NOPE + ROPE).reshape(P, -1)
        return np.concatenate([uq, cols(a["mla_w_ukv"][l], j * P, P).reshape(P, -1)], 1)
    if kind in ("pa", "pb", "pc"):
        return cols(a["w_" + kind][l], 2 * P * j, 2 * P).reshape(P, -1)
    return cols(a["w_out"][l], P * j, P).reshape(P, -1)


def lay_out(a):
    a = {k: np.asarray(v) for k, v in a.items()}
    cs, decay = constants()
    cs[:, CST["c"][0]:CST["c"][1]] = columns(a["c"][0], DT)
    cs[:, CST["final_g"][0]:CST["final_g"][1]] = columns(a["final_g"], DT)
    cur = np.zeros((DEPTH, P, N_CUR), np.float32)
    nxt = np.zeros((DEPTH + 1, P, N_NXT), np.float32)
    b = columns(a["b_mod"].reshape(DEPTH, 3, D_MODEL), DT)
    for l in range(DEPTH):
        def put(name, v):
            cur[l][:, CUR[name][0]:CUR[name][1]] = v

        put("b_gate", b[l, 2])
        put("logits", a["hg_lb_logits"].reshape(DEPTH, HG_HEADS, HG_DK).transpose(2, 0, 1).reshape(P, -1))
        put("sel", [float(1 <= j <= l) for j in range(DEPTH)])
        put("onorm", a["hg_onorm_g"][l][:, None])
        put("g_cq", columns(a["mla_g_cq"][l], CQT))
        put("g_ckv", columns(a["mla_g_ckv"][l], CKT))
    for l in range(DEPTH + 1):
        m = (l + 1) % DEPTH if l < DEPTH else 0
        nxt[l] = np.concatenate([columns(a["norm_g"][m], DT), b[m, 0], b[m, 1]], 1)
    w_stream = np.stack([np.concatenate([np.ascontiguousarray(item_weights(it, l, a)).ravel() for it in ITEMS])
                         for l in range(DEPTH)])
    wm = a["w_mod"].reshape(DEPTH, D_MODEL, 3, D_MODEL)
    mixed = np.stack([np.stack([wm[l][:, 2], wm[(l + 1) % DEPTH][:, 0], wm[(l + 1) % DEPTH][:, 1]], 1) for l in range(DEPTH)])
    w_mod = mixed.reshape(DEPTH, DT, P, MOD_SECTIONS, MOD_W).transpose(0, 3, 1, 2, 4).reshape(DEPTH, MOD_SECTIONS * DT, P, MOD_W)
    w_mod_first = wm[0][:, :2].reshape(DT, P, 2, D_MODEL).transpose(2, 0, 1, 3).reshape(2 * DT, P, D_MODEL)
    return {
        "x_t": a["x"][0].T.reshape(DT, P, SEQ).transpose(1, 0, 2),
        "positions": a["positions"],
        "cst": cs, "decay": decay, "params_cur": cur, "params_nxt": nxt,
        "w_stream": w_stream, "w_mod": w_mod, "w_mod_first": w_mod_first,
    }


def kernel(**inputs):
    import concourse.bacc as _bacc
    from concourse.bass_utils import run_bass_kernel_spmd as _run

    arrays = {n: np.ascontiguousarray(v) for n, v in lay_out(inputs).items()}
    nc = _bacc.Bacc("TRN2", target_bir_lowering=False, num_devices=1, dynamic_dma_scratch_size=1024)
    ins = [nc.dram_tensor(n, list(v.shape), mybir.dt.from_np(v.dtype), kind="ExternalInput").ap() for n, v in arrays.items()]
    out = nc.dram_tensor("out_t", [P, DT, SEQ], F32, kind="ExternalOutput").ap()
    build(nc, *ins, out)
    r = _run(nc, [arrays], core_ids=[0])
    out = r.results[0]["out_t"]
    return np.ascontiguousarray(out.transpose(1, 0, 2).reshape(D_MODEL, SEQ).T).reshape(1, SEQ, D_MODEL)
```

```python
from contextlib import ExitStack

import concourse.bass as bass
import numpy as np
from concourse import mybir

F32 = mybir.dt.float32
F32R = mybir.dt.float32r
BF16 = mybir.dt.bfloat16
I32 = mybir.dt.int32
U32 = mybir.dt.uint32
ACT = mybir.ActivationFunctionType
ALU = mybir.AluOpType
AX = mybir.AxisListType

P = 128
D_MODEL, SEQ, DEPTH = 1024, 512, 2
DT = D_MODEL // P
CH = SEQ // P
HG_HEADS, HG_DK = 4, 128
MLA_HEADS, NOPE, ROPE, MLA_DV, D_C, D_CQ = 8, 64, 32, 64, 256, 768
RET_HEADS, RET_DK, RET_DV = 4, 64, 128
CQT, CKT = D_CQ // P, D_C // P
EPS = 1e-6
MLA_SCALE = float(NOPE + ROPE) ** -0.5
SIG_MIN = -44.0
TWO_PI = (6.28125, 0.0019340515136718750, 1.2556659146e-6)
LOG_FLOOR = 1e-20
assert np.exp(SIG_MIN) > LOG_FLOOR
ROUND = 12582912.0
PI_BELOW = 3.1415925
PRO_RING = 8
assert 2 * DT - PRO_RING >= DT
TABLE_SET = "natural_log_exp_and_others"
LINKS = {"act": 100, "dve": 60}
LEVELS = (64, 32, 16, 8, 4)
BASE = 4

OFF = {}
_at = 0
for _n, _s in (("a_q", 512), ("a_f", 512), ("a_i", 512), ("a_g", 512), ("b_cq", D_CQ), ("b_ckv", D_C), ("b_kr", ROPE),
               ("b_g", 512), ("c_q", 256), ("c_k", 256), ("c_v", 512), ("c_g", 512),
               ("m_a", D_MODEL), ("m_b", D_MODEL), ("m_c", D_MODEL)):
    OFF[_n] = _at
    _at += _s

NORM_TILES = {"cq_norm": range(CQT // 2), "cq_rest": range(CQT // 2, CQT), "ckv_norm": range(CKT)}
MERGES = ("ma", "mb", "mc")

RING = 3
SLOT = DT * P


def merge_items(b):
    order = [("m", 0), ("m", 1), ("m", 2), ("p", 0), ("m", 3), ("m", 4), ("p", 1), ("m", 5), ("m", 6), ("p", 2),
             ("m", 7), ("p", 3)]
    return [(k + b, j) for k, j in order]


def tiles_of(item):
    kind = item[0]
    if kind in ("pa", "pb", "pc"):
        return [(4, P, 0, 2 * P), (4, P, P, 2 * P)]
    if kind == "mla":
        return [(CQT, P, 0, P), (CKT, P, CQT * P, P)]
    return [(DT, P, 0, P)]


def elements_of(item):
    return sum(nk * m for nk, m, _, _ in tiles_of(item))


def build_schedule():
    s = [("norm",)]

    def item(kind, j):
        s.append(("item", kind, j))

    def hg_first(h):
        return ([("hg_lv", h - 1, 4), ("hg_lv", h - 1, 5)],
                [("hg_lv", h - 1, 6), ("hg_lv", h - 1, 7), ("hz", h, 1), ("hz", h, 2), ("hg_cross", h - 1)],
                [("hz", h, 3), ("hg_pv", h - 1), ("hg_lv", h, 0), ("hg_lv", h, 1), ("hg_out", h - 1)],
                [("hg_v", h), ("hg_lv", h, 2), ("hg_lv", h, 3)])

    for h in range(HG_HEADS):
        for kind, steps in zip(("f", "q", "i", "g"), hg_first(h)):
            item(kind, h)
            if (kind, h) == ("i", 0):
                item("cq", 0)
            s += [t for t in steps if t[1] >= 0]
    h = HG_HEADS
    item("cq", 1)
    s += hg_first(h)[0]
    item("cq", 2)
    s += [t for t in hg_first(h)[1] if t[0] != "hz"]
    item("cq", 3)
    s += [("hg_pv", h - 1)]
    item("cq", 4)
    s += [("hg_out", h - 1)]
    item("cq", 5)
    item("ckv", 0)
    s.append(("cq_norm",))
    item("ckv", 1)
    s.append(("cq_rest",))
    item("kr", 0)
    s.append(("ckv_norm",))
    ma = merge_items("a")
    item(*ma[0])
    s.append(("kr_rope",))
    for it in ma[1:-3]:
        item(*it)
    item("mla", 0)
    item(*ma[-3])
    s.append(("mla_qk", 0))
    item("mla", 1)
    item(*ma[-2])
    item(*ma[-1])
    item("bg", 0)
    for h in range(MLA_HEADS):
        s += [("mla_s", h, 3), ("mla_s", h, 2)]
        if h:
            s.append(("mla_pv", h - 1))
        if h + 1 < MLA_HEADS:
            s.append(("mla_qk", h + 1))
        else:
            s.append(("ret_rope", "rq", 0))
        if h % 2 == 1 and h + 1 < MLA_HEADS:
            item("bg", (h + 1) // 2)
        s += [("mla_t", h, 3), ("mla_t", h, 2), ("mla_s", h, 1), ("mla_s", h, 0)]
        item(*(("mla", h + 2) if h + 2 < MLA_HEADS else ("rq", h + 2 - MLA_HEADS)))
        s += [("mla_t", h, 1), ("mla_t", h, 0)]
    rest = [("rk", 0), ("rk", 1)] + [("rv", h) for h in range(RET_HEADS)]
    after = [("ret_rope", "rq", 1), ("ret_rope", "rk", 0), ("ret_rope", "rk", 1)] + [("ret_v", h) for h in range(RET_HEADS)]
    for it, t in zip(rest, after):
        item(*it)
        if it == ("rk", 0):
            s.append(("mla_pv", MLA_HEADS - 1))
        s.append(t)
    mb = merge_items("b")
    for h in range(RET_HEADS):
        s += [("ret_s", h, 0), ("ret_s", h, 1)]
        item(*mb[3 * h])
        if h == 0:
            s.append(after[-1])
        s += [("ret_s", h, 2), ("ret_s", h, 3)]
        item("cg", h)
        s += [("ret_pv", h)]
        item(*mb[3 * h + 1])
        if h + 1 < RET_HEADS:
            s.append(("ret_out", h))
        item(*mb[3 * h + 2])
    s.append(("ret_out", RET_HEADS - 1))
    for k, j in merge_items("c"):
        item(k, j)
    for j in range(DT):
        item("wo", j)
    s.append(("end",))
    return s


SCHEDULE = build_schedule()
ITEMS = [s[1:] for s in SCHEDULE if s[0] == "item"]
N_ITEMS = len(ITEMS)
ITEM_AT = {it: n for n, it in enumerate(ITEMS)}
ITEM_BASE = np.concatenate([[0], np.cumsum([elements_of(it) * P for it in ITEMS])]).astype(int).tolist()
assert N_ITEMS % RING == 0

STREAM = ("st0", "st1")
BANKS = ("st0", "st1", "s0", "s1", "w0", "w1", "o", "misc")


def build_uses():
    count = dict.fromkeys(BANKS, 0)
    uses = {}

    def use(bank, key):
        uses[key] = (bank, count[bank])
        count[bank] += 1

    out = 0
    for s in SCHEDULE:
        kind = s[0]
        if kind == "norm":
            use("misc", ("ssq",))
        elif kind == "item":
            for t in range(len(tiles_of(s[1:]))):
                use(STREAM[out % 2], (s[1:], t))
                out += 1
        elif kind == "hg_lv":
            if 1 <= s[2] <= 6:
                use(("s0", "s1")[(s[2] - 1) % 2], ("lv", s[1], s[2] - 1))
            if s[2] == 7:
                use("w0", ("cross0", s[1]))
                use("w1", ("cross1", s[1]))
        elif kind in ("hg_pv", "ret_pv"):
            use("o", (kind, s[1]))
        elif kind in ("hg_out", "ret_out", "cq_norm", "ckv_norm", "ret_rope", "ret_v"):
            use("misc", s)
        elif kind == "hg_v":
            use("w0", s)
        elif kind == "mla_qk":
            use("misc", ("mla_v", s[1]))
        elif kind == "mla_s":
            use(("s0", "s1")[s[2] % 2], s)
        elif kind == "mla_t":
            use(("w0", "w1")[s[2] % 2], s)
        elif kind == "mla_pv":
            use("o", s)
        elif kind == "ret_s":
            use(("s0", "s1")[s[2] % 2], s)
        elif kind == "mod_sum":
            use("w1", s)
    return uses, count


MOD_W = 512
MOD_SECTIONS = D_MODEL * 3 // MOD_W


def add_mod_steps():
    steps = []
    for sec in range(MOD_SECTIONS):
        for k in range(DT):
            steps.append(("mod_acc", sec, k))
        steps.append(("mod_sum", sec))
    out = []
    n = 0
    total = N_ITEMS - 12
    for s in SCHEDULE:
        out.append(s)
        if s[0] == "item":
            n += 1
            while steps and len(steps) > (total - n) * (MOD_SECTIONS * (DT + 1)) / total:
                out.append(steps.pop(0))
    assert not steps
    return out


SCHEDULE = add_mod_steps()
USES, BANK_USES = build_uses()

EARLY = ("hz", "hg_lv", "mod_acc")
LATER = ("hg_v", "hg_out", "mla_pv", "ret_out")


def mixers_first():
    out, group, later, i = [], [], [], -1
    for s in SCHEDULE + [("item",)]:
        if s[0] == "item":
            out += [t for t in group if t[0] in EARLY]
            out += later + [t for t in group if t[0] == "item"]
            out += [t for t in group if t[0] not in EARLY + LATER + ("item",)]
            later = [t for t in group if t[0] in LATER]
            i += 1
            group = [s]
            if i < N_ITEMS:
                out.append(("split", i + RING - 1))
        else:
            group.append(s)
    assert not later
    return out


MIXERS_FIRST = mixers_first()

CUR = {}
_at = 0
for _n, _s in (("b_gate", DT), ("logits", DEPTH * HG_HEADS), ("sel", DEPTH), ("onorm", 1), ("g_cq", CQT), ("g_ckv", CKT)):
    CUR[_n] = (_at, _at + _s)
    _at += _s
N_CUR = _at
NXT = {"norm_g": (0, DT), "b_shift": (DT, 2 * DT), "b_scale": (2 * DT, 3 * DT)}
N_NXT = 3 * DT
CST = {}
_at = 0
for _n, _s in (("ident", P), ("ones", P), ("perm_ret", P), ("m64", P), ("m32", P), ("m16", P),
               ("m8", P), ("m4", P), ("mbase", P), ("reset", SEQ), ("neg", P), ("inv_mla", 1), ("inv_ret", 1),
               ("eps", 1), ("one", 1), ("half_pi", 1), ("c", DT), ("final_g", DT)):
    CST[_n] = (_at, _at + _s)
    _at += _s
N_CST = _at



def bank_of(key):
    return USES[key][0]


GATES = HG_HEADS * 2 + MLA_HEADS // 2 + RET_HEADS
PAIRS = MLA_HEADS // 2
PER_LAYER = {
    **{f"{s}_{b}": n for s in ("full", "free") for b, n in BANK_USES.items()},
    **{f"raw_in{i}": 16 * (N_ITEMS // RING) for i in range(RING)},
    **{f"mod_in{i}": 16 * (MOD_SECTIONS * DT // 2) for i in range(2)},
    "mod_done": MOD_SECTIONS * DT, "params_in": 32, "decay_in": 16, "lb_d_ready": 1, "lb_e_ready": 1,
    "w_hi_ready": N_ITEMS, "w_lo_ready": N_ITEMS,
    "sq_sum_ready": 1, "norm_t": DT, "norm_hi": DT, "h_ready": DT, "x_sq": DT, "x_sum": DT - 1,
    "mg_t": DT, "mg_hi_ready": DT, "mg_ready": DT,
    "rstd_ready": 3 + HG_HEADS + RET_HEADS + MLA_HEADS,
    "gate_sig": GATES, "silu_done": GATES, "sigma_ready": 3 * DT,
    "hz_ln": HG_HEADS, "hz_u": HG_HEADS, "hz_s": HG_HEADS, "hz_f": HG_HEADS, "hz_l": HG_HEADS, "b_ready": HG_HEADS,
    "d_ready": 7 * HG_HEADS, "e_ready": 7 * HG_HEADS, "x_built": 7 * HG_HEADS,
    "o_sq_ready": HG_HEADS + RET_HEADS,
    "y_t_ready": HG_HEADS + PAIRS + RET_HEADS, "y_hi_ready": HG_HEADS + PAIRS + RET_HEADS,
    "y_ready": HG_HEADS + PAIRS + RET_HEADS,
    "cq_sq": CQT + CKT, "cq_sum": CQT + CKT, "cqn_t": CQT + CKT, "cqn_hi": CQT + CKT, "cqn_ready": CQT + CKT,
    "q_ready": MLA_HEADS, "k_ready": MLA_HEADS, "p_max": CH * MLA_HEADS, "ret_qk_ready": 4,
    "act_link": LINKS["act"], "dve_link": LINKS["dve"],
}


class Counter:

    def __init__(self, eng, layer, per_layer):
        self.eng, self.layer, self.per_layer = eng, layer, per_layer
        self.asked, self.own = {}, {}
        self.base, self.value = {}, eng.alloc_register(name="wait_value")

    def at(self, sem, k):
        self.asked[id(sem)] = max(k, self.asked.get(id(sem), 0))
        n = self.per_layer[id(sem)]
        if n not in self.base:
            self.base[n] = self.eng.alloc_register(name=f"layer_times_{n}")
            self.eng.reg_mul(self.base[n], self.layer, n)
        self.eng.reg_add(self.value, self.base[n], k)
        return self.value

    def new(self, sem, k):
        return self.asked.get(id(sem), 0) < k

    def use(self, banks, key):
        b, k = USES[key]
        return self.at(banks[b], k + 1)

    def made(self, sem):
        self.own[id(sem)] = self.own.get(id(sem), 0) + 1
        return self.at(sem, self.own[id(sem)])


def build(nc, x_t, positions, cst, decay, params_cur, params_nxt, w_stream, w_mod, w_mod_first, out_t):
    ctx = ExitStack()
    with ctx:
        def sb(name, shape, dt=F32):
            return ctx.enter_context(nc.sbuf_tensor(name, shape, dt))

        def sem(name):
            return ctx.enter_context(nc.semaphore(name))

        x = sb("x", [P, DT, SEQ])
        h_hi = sb("h_hi", [P, DT, SEQ], F32R)
        h_lo = sb("h_lo", [P, DT, SEQ], F32R)
        raw = sb("raw", [P, RING, SLOT])
        w_hi = sb("w_hi", [P, RING, SLOT], F32R)
        w_lo = sb("w_lo", [P, RING, SLOT], F32R)
        mod_w = sb("mod_w", [P, 2, MOD_W])
        mod_acc = sb("mod_acc", [P, MOD_W])
        cs = sb("cs", [P, N_CST])
        cos_mla, sin_mla = sb("cos_mla", [P, SEQ]), sb("sin_mla", [P, SEQ])
        cos_ret, sin_ret = sb("cos_ret", [P, SEQ]), sb("sin_ret", [P, SEQ])
        ident_bf, neg_bf = sb("ident_bf", [P, P], BF16), sb("neg_bf", [P, P], BF16)
        v_ones = sb("v_ones", [P, CH, 3 * MLA_DV])
        rstd = sb("rstd", [P, SEQ])
        gate_x, gate_t = sb("gate_x", [P, 2, SEQ]), sb("gate_t", [P, 2, SEQ])
        t1, t2, y_t = sb("t1", [P, SEQ]), sb("t2", [P, SEQ]), sb("y_t", [P, SEQ])
        sq_t, sq_sum = sb("sq_t", [P, SEQ]), sb("sq_sum", [P, SEQ])
        cur = sb("cur", [P, N_CUR])
        nxt = sb("nxt", [P, N_NXT])
        shift, scale_g, gate = sb("shift", [P, DT]), sb("scale_g", [P, DT]), sb("gate", [P, DT])
        cond, cond_t = sb("cond", [P, DT]), sb("cond_t", [P, DT])
        lb, one_lb = sb("lb", [P, HG_HEADS]), sb("one_lb", [P, HG_HEADS])
        lb_e = sb("lb_e", [P, DEPTH, HG_HEADS])
        lb_t = sb("lb_t", [P, HG_HEADS])
        centre = sb("centre", [P, SEQ // BASE])
        g_last = sb("g_last", [P, CH])
        carry = sb("carry", [P, 1])
        neg_max = sb("neg_max", [P, CH])

        arena = nc.sbuf_base + (-nc.sbuf_base) % 64
        KB = 1024

        def at(name, offset, shape, dt=F32):
            return nc.alloc_sbuf_tensor_at(name, shape, dt, offset=arena + offset)

        hg_q, hg_k, hg_b = at("hg_q", 0, [P, 2, SEQ]), at("hg_k", 4 * KB, [P, 2, SEQ]), at("hg_b", 8 * KB, [P, 2, SEQ])
        hg_e, hg_x = at("hg_e", 12 * KB, [P, 2, SEQ]), at("hg_x", 16 * KB, [P, 2, SEQ])
        hg_at = (at("hg_at0", 20 * KB, [P, CH, SEQ]), at("hg_at1", 40 * KB, [P, CH, SEQ]))
        hg_kd = at("hg_kd", 28 * KB, [P, 3 * P])
        hg_qc = at("hg_qc", 64 * KB, [P, 3, 3 * P])
        hg_vt = at("hg_vt", 69 * KB, [P, SEQ])
        hg_v = at("hg_v", 71 * KB, [P, 2, CH, P])
        hg_g = at("hg_g", 75 * KB, [P, 2, SEQ])
        hz_a, hz_b, hz_c = at("hz_a", 79 * KB, [P, SEQ]), at("hz_b", 81 * KB, [P, SEQ]), at("hz_c", 83 * KB, [P, SEQ])
        cq_hi, cq_lo = at("cq_hi", 0, [P, CQT, SEQ], F32R), at("cq_lo", 12 * KB, [P, CQT, SEQ], F32R)
        ckv_hi, ckv_lo = at("ckv_hi", 24 * KB, [P, CKT, SEQ], F32R), at("ckv_lo", 28 * KB, [P, CKT, SEQ], F32R)
        cq_raw, ckv_raw = at("cq_raw", 32 * KB, [P, CQT, SEQ]), at("ckv_raw", 44 * KB, [P, CKT, SEQ])
        mla_q, mla_kv = at("mla_q", 64 * KB, [P, 2, SEQ]), at("mla_kv", 68 * KB, [P, 2, SEQ])
        mla_p, mla_pt = at("mla_p", 72 * KB, [P, 2, SEQ]), at("mla_pt", 76 * KB, [P, CH, SEQ])
        mla_g = at("mla_g", 84 * KB, [P, 2, SEQ])
        ckv_sum = at("ckv_sum", 88 * KB, [P, SEQ])
        k_rope = at("k_rope", 90 * KB, [P, SEQ])
        o_sq = at("o_sq", 90 * KB, [P, SEQ])
        ret_q, ret_k = at("ret_q", 0, [P, 2, SEQ]), at("ret_k", 4 * KB, [P, 2, SEQ])
        ret_v = at("ret_v", 8 * KB, [P, RET_HEADS, CH, P])
        ret_sc = at("ret_sc", 16 * KB, [P, CH, SEQ])
        ret_decay = at("ret_decay", 24 * KB, [P, RET_HEADS, SEQ])
        yc_hi, yc_lo = at("yc_hi", 64 * KB, [P, CH, SEQ], F32R), at("yc_lo", 72 * KB, [P, CH, SEQ], F32R)
        ret_vt = (at("ret_vt0", 80 * KB, [P, SEQ]), at("ret_vt1", 88 * KB, [P, SEQ]))
        ret_g = at("ret_g", 82 * KB, [P, SEQ])
        merged = at("merged", 32 * KB, [P, DT, SEQ])
        y_hi, y_lo = at("y_hi", 48 * KB, [P, CH, SEQ], F32R), at("y_lo", 56 * KB, [P, CH, SEQ], F32R)
        sigma = at("sigma", 84 * KB, [P, 3, SEQ])
        arena_end = arena + 92 * KB
        assert arena_end <= nc.sbuf_usable_end, (arena_end, nc.sbuf_usable_end)
        mg_hi, mg_lo = at("mg_hi", 0, [P, DT, SEQ], F32R), at("mg_lo", 16 * KB, [P, DT, SEQ], F32R)
        pro_w = at("pro_w", 0, [P, PRO_RING, D_MODEL])
        pro_acc = at("pro_acc", 32 * KB, [P, 2 * D_MODEL])
        pos_i = at("pos_i", 40 * KB, [P, SEQ], I32)
        pos_f, ang, turn = at("pos_f", 42 * KB, [P, SEQ]), at("ang", 44 * KB, [P, SEQ]), at("turn", 46 * KB, [P, SEQ])
        red = at("red", 48 * KB, [P, 4, SEQ])
        o_t = at("o_t", 0, [P, DT, SEQ])

        def c(name):
            a, b = CST[name]
            return cs[:, a:b]

        def pc(name):
            a, b = CUR[name]
            return cur[:, a:b]

        def pn(name):
            a, b = NXT[name]
            return nxt[:, a:b]

        def diagonal(t):
            a = t[:, :, 0:P]
            steps = [list(v) for v in a.ap]
            steps[-2][0] += P
            return bass.AP(tensor=a.tensor, offset=a.offset, ap=steps)

        ident, ones, eps, one = c("ident"), c("ones"), c("eps"), c("one")

        bank = {n: ctx.enter_context(nc.psum_tensor("ps_" + n, [P, SEQ], F32)) for n in BANKS}

        per_layer = {}

        def signal(name):
            s = sem(name)
            per_layer[id(s)] = PER_LAYER[name]
            return s

        full = {n: signal("full_" + n) for n in BANKS}
        free = {n: signal("free_" + n) for n in BANKS}
        raw_in = [signal(f"raw_in{i}") for i in range(RING)]
        mod_in = [signal(f"mod_in{i}") for i in range(2)]
        w_hi_ready = signal("w_hi_ready")
        w_lo_ready = signal("w_lo_ready")
        sq_sum_ready = signal("sq_sum_ready")
        act_link, dve_link = signal("act_link"), signal("dve_link")
        rstd_ready = signal("rstd_ready")
        norm_t, norm_hi, h_ready = signal("norm_t"), signal("norm_hi"), signal("h_ready")
        gate_sig, silu_done, sigma_ready = (signal(n) for n in ("gate_sig", "silu_done", "sigma_ready"))
        hz_ln, hz_u, hz_s, hz_f, hz_l = (signal(n) for n in ("hz_ln", "hz_u", "hz_s", "hz_f", "hz_l"))
        b_ready, d_ready, e_ready, x_built = (signal(n) for n in ("b_ready", "d_ready", "e_ready", "x_built"))
        o_sq_ready, y_t_ready, y_hi_ready, y_ready = (signal(n) for n in ("o_sq_ready", "y_t_ready", "y_hi_ready", "y_ready"))
        cq_sq, cq_sum, cqn_t, cqn_hi, cqn_ready = (signal(n) for n in ("cq_sq", "cq_sum", "cqn_t", "cqn_hi", "cqn_ready"))
        q_ready, k_ready, p_max = (signal(n) for n in ("q_ready", "k_ready", "p_max"))
        ret_qk_ready, decay_in = signal("ret_qk_ready"), signal("decay_in")
        mg_t, mg_hi_ready, mg_ready = (signal(n) for n in ("mg_t", "mg_hi_ready", "mg_ready"))
        x_sq, x_sum = signal("x_sq"), signal("x_sum")
        params_in, lb_d_ready, lb_e_ready = (signal(n) for n in ("params_in", "lb_d_ready", "lb_e_ready"))
        mod_done = signal("mod_done")
        names = ("const_in", "x_in", "pos_in", "par_in", "cond_e", "pro_link", "pro_mod_done", "pro_mod_sum",
                 "angles", "tables", "pro_sq", "pro_sum", "fin_sum", "fin_link", "fin_rstd", "fin_out", "stored")
        (const_in, x_in, pos_in, par_in, cond_e, pro_link, pro_mod_done, pro_mod_sum, angles, tables, pro_sq,
         pro_sum, fin_sum, fin_link, fin_rstd, fin_out, stored) = (sem(n) for n in names)
        pro_in = [sem(f"pro_in{i}") for i in range(PRO_RING)]

        block = ctx.enter_context(nc.Block())

        @block.sync
        def _(sp):
            sp.dma_start(cs[:], cst).then_inc(const_in, 16)
            for j in range(0, DT, 2):
                sp.dma_start(x[:, j:j + 2, :], x_t[:, j:j + 2, :]).then_inc(x_in, 16)
            with sp.Fori(0, DEPTH) as layer:
                e = Counter(sp, layer, per_layer)
                for i, it in enumerate(ITEMS):
                    n = elements_of(it)
                    sp.wait_ge(w_lo_ready, e.at(w_lo_ready, i + 1))
                    src = w_stream[layer, ITEM_BASE[i]:ITEM_BASE[i] + P * n].rearrange("(p n) -> p n", p=P)
                    sp.dma_start(raw[:, i % RING, 0:n], src).then_inc(raw_in[i % RING], 16)
            for j in range(DT):
                sp.wait_ge(fin_out, j + 1)
                sp.dma_start(out_t[:, j, :], o_t[:, j, :]).then_inc(stored, 16)
            sp.wait_ge(stored, 16 * DT)

        @block.gpsimd
        def _(pool):
            pool.sem_inc(w_lo_ready, RING)
            for j in range(DT):
                pool.wait_ge(pro_sq, j + 1)
                src = (sq_t, o_sq)[j % 2][:]
                if j == 0:
                    nc.gpsimd.tensor_copy(sq_sum[:], src).then_inc(pro_sum, 1)
                else:
                    nc.gpsimd.tensor_tensor(sq_sum[:], sq_sum[:], src, ALU.add).then_inc(pro_sum, 1)
                pool.wait_ge(pro_sum, j + 1)
            with pool.Fori(0, DEPTH) as layer:
                e = Counter(pool, layer, per_layer)
                for i, it in enumerate(ITEMS):
                    n = elements_of(it)
                    pool.wait_ge(w_hi_ready, e.at(w_hi_ready, i + 1))
                    nc.gpsimd.tensor_tensor(w_lo[:, i % RING, 0:n], raw[:, i % RING, 0:n],
                                            w_hi[:, i % RING, 0:n].bitcast(F32), ALU.subtract).then_inc(w_lo_ready, 1)

        @block.tensor
        def _(pe):
            pe.wait_ge(const_in, 16)
            for j in range(2 * DT):
                if j % DT == 0:
                    pe.wait_ge(pro_mod_done, DT + j)
                last = nc.tensor.matmul(bank["misc"][:, j:j + 1], pro_acc[:, j * P:(j + 1) * P], ones[:, 0:1],
                                        start=True, stop=True)
            last.then_inc(pro_mod_sum, 1)
            with pe.Fori(0, DEPTH) as layer:
                e = Counter(pe, layer, per_layer)

                def take(key):
                    b, k = USES[key]
                    if k > 0:
                        if e.new(free[b], k):
                            pe.wait_ge(free[b], e.at(free[b], k))
                    return bank[b]

                def done(ins, key):
                    ins.then_inc(full[bank_of(key)], 1)

                def moving(kind, t, k):
                    if kind == "pa":
                        if e.new(y_ready, k + 1):
                            pe.wait_ge(y_ready, e.at(y_ready, k + 1))
                        return y_hi[:, k, :], y_lo[:, k, :]
                    if kind == "pb":
                        if e.new(y_ready, CH + k + 1):
                            pe.wait_ge(y_ready, e.at(y_ready, CH + k + 1))
                        return y_hi[:, k, :], y_lo[:, k, :]
                    if kind == "pc":
                        if e.new(y_ready, 2 * CH + k + 1):
                            pe.wait_ge(y_ready, e.at(y_ready, 2 * CH + k + 1))
                        return yc_hi[:, k, :], yc_lo[:, k, :]
                    if kind == "mla" and t == 0:
                        if e.new(cqn_ready, k + 1):
                            pe.wait_ge(cqn_ready, e.at(cqn_ready, k + 1))
                        return cq_hi[:, k, :], cq_lo[:, k, :]
                    if kind == "mla":
                        if e.new(cqn_ready, CQT + k + 1):
                            pe.wait_ge(cqn_ready, e.at(cqn_ready, CQT + k + 1))
                        return ckv_hi[:, k, :], ckv_lo[:, k, :]
                    if kind == "wo":
                        if e.new(mg_ready, k + 1):
                            pe.wait_ge(mg_ready, e.at(mg_ready, k + 1))
                        return mg_hi[:, k, :], mg_lo[:, k, :]
                    if e.new(h_ready, k + 1):
                        pe.wait_ge(h_ready, e.at(h_ready, k + 1))
                    return h_hi[:, k, :], h_lo[:, k, :]

                def first_items():
                    dst = [take((it, 0)) for it in ITEMS[:2]]
                    behind = 3
                    for step in range(DT + behind):
                        for i, k in ((0, step), (1, step - behind)):
                            if not 0 <= k < DT:
                                continue
                            if k == 0:
                                pe.wait_ge(w_lo_ready, e.at(w_lo_ready, RING + i + 1))
                            hi, lo = moving("f", 0, k)
                            wh, wl = w_hi[:, i, k * P:(k + 1) * P], w_lo[:, i, k * P:(k + 1) * P]
                            nc.tensor.matmul(dst[i][:], wh, hi, start=(k == 0), stop=False)
                            nc.tensor.matmul(dst[i][:], wh, lo, start=False, stop=False)
                            last = nc.tensor.matmul(dst[i][:], wl, hi, start=False, stop=(k == DT - 1))
                            if k == DT - 1:
                                done(last, (ITEMS[i], 0))

                def item(it):
                    i = ITEM_AT[it]
                    pe.wait_ge(w_lo_ready, e.at(w_lo_ready, RING + i + 1))
                    for t, (nk, m, first, step) in enumerate(tiles_of(it)):
                        dst = take((it, t))
                        for k in range(nk):
                            hi, lo = moving(it[0], t, k)
                            a = first + k * step
                            wh, wl = w_hi[:, i % RING, a:a + m], w_lo[:, i % RING, a:a + m]
                            nc.tensor.matmul(dst[0:m, :], wh, hi, start=(k == 0), stop=False)
                            nc.tensor.matmul(dst[0:m, :], wh, lo, start=False, stop=False)
                            last = nc.tensor.matmul(dst[0:m, :], wl, hi, start=False, stop=(k == nk - 1))
                        done(last, (it, t))

                def transposes(key, src):
                    dst = take(key)
                    for k in range(CH):
                        last = nc.tensor.transpose(dst[:, k * P:(k + 1) * P], src(k), ident)
                    done(last, key)

                def swap_halves(key, perm, src, rows):
                    dst = take(key)
                    done(nc.tensor.matmul(dst[0:rows, :], perm[0:rows, 0:rows], src, start=True, stop=True), key)

                def column_sums(key, src):
                    dst = take(key)
                    done(nc.tensor.matmul(dst[:], ones, src, start=True, stop=True), key)

                def weighted_values(key, values, weights):
                    dst = take(key)
                    for k in range(CH):
                        last = nc.tensor.matmul(dst[:, k * P:], values(k), weights[:, k, k * P:],
                                                start=(k == 0), stop=(k == CH - 1))
                    done(last, key)

                for s in SCHEDULE:
                    kind = s[0]
                    if kind == "norm":
                        pe.wait_ge(sq_sum_ready, e.at(sq_sum_ready, 1))
                        column_sums(("ssq",), sq_sum[:])
                    elif kind == "item":
                        if ITEM_AT[s[1:]] == 0:
                            first_items()
                        elif ITEM_AT[s[1:]] > 1:
                            item(s[1:])
                    elif kind == "hg_v":
                        pe.wait_ge(free[bank_of((("i", s[1]), 0))], e.use(free, (("i", s[1]), 0)))
                        transposes(s, lambda k: hg_vt[:, k * P:(k + 1) * P])
                    elif kind == "hg_lv" and 1 <= s[2] <= 6:
                        h, n = s[1], s[2] - 1
                        pe.wait_ge(x_built, e.at(x_built, 7 * h + n + 1))
                        dst = take(("lv", h, n))
                        left, right = (hg_x[:, n % 2, :], hg_x[:, n % 2, :]) if n < 5 else (hg_x[:, 0, :], hg_x[:, 1, :])
                        for k in range(CH):
                            r = slice(k * P, (k + 1) * P)
                            last = nc.tensor.matmul(dst[:, r], left[:, r], right[:, r], start=True, stop=True)
                        done(last, ("lv", h, n))
                    elif kind == "hg_lv" and s[2] == 7:
                        h = s[1]
                        pe.wait_ge(x_built, e.at(x_built, 7 * h + 7))
                        d0 = take(("cross0", h))
                        nc.tensor.matmul(d0[:, 0:3 * P], hg_kd[:, 0:P], hg_qc[:, 0, :], start=True, stop=True)
                        done(nc.tensor.matmul(d0[:, 3 * P:], hg_kd[:, 2 * P:3 * P], hg_qc[:, 2, 0:P], start=True, stop=True),
                             ("cross0", h))
                        d1 = take(("cross1", h))
                        done(nc.tensor.matmul(d1[:, 0:2 * P], hg_kd[:, P:2 * P], hg_qc[:, 1, 0:2 * P], start=True, stop=True),
                             ("cross1", h))
                    elif kind == "hg_pv":
                        h = s[1]
                        pe.wait_ge(free[bank_of(("hg_v", h))], e.use(free, ("hg_v", h)))
                        pe.wait_ge(free[bank_of(("lv", h, 4))], e.use(free, ("lv", h, 4)))
                        pe.wait_ge(free[bank_of(("lv", h, 5))], e.use(free, ("lv", h, 5)))
                        pe.wait_ge(free[bank_of(("cross0", h))], e.use(free, ("cross0", h)))
                        pe.wait_ge(free[bank_of(("cross1", h))], e.use(free, ("cross1", h)))
                        weighted_values(s, lambda k: hg_v[:, h % 2, k, :], hg_at[h % 2])
                    elif kind in ("hg_out", "ret_out"):
                        pe.wait_ge(o_sq_ready, e.at(o_sq_ready, (0 if kind == "hg_out" else HG_HEADS) + s[1] + 1))
                        column_sums(s, o_sq[:])
                    elif kind in ("cq_norm", "ckv_norm"):
                        pe.wait_ge(cq_sum, e.at(cq_sum, CQT if kind == "cq_norm" else CQT + CKT))
                        column_sums(s, (sq_sum if kind == "cq_norm" else ckv_sum)[:])
                    elif kind == "ret_rope":
                        pe.wait_ge(free[bank_of((s[1:], 0))], e.use(free, (s[1:], 0)))
                        swap_halves(s, c("perm_ret"), (ret_q if s[1] == "rq" else ret_k)[:, s[2], :], P)
                    elif kind == "ret_v":
                        pe.wait_ge(free[bank_of((("rv", s[1]), 0))], e.use(free, (("rv", s[1]), 0)))
                        transposes(s, lambda k: ret_vt[s[1] % 2][:, k * P:(k + 1) * P])
                    elif kind == "mla_qk":
                        h = s[1]
                        pe.wait_ge(free[bank_of((("mla", h), 1))], e.use(free, (("mla", h), 1)))
                        transposes(("mla_v", h), lambda k: mla_kv[:, h % 2, k * P:(k + 1) * P])
                    elif kind == "mla_s":
                        h, qi = s[1:]
                        if e.new(q_ready, h + 1):
                            pe.wait_ge(q_ready, e.at(q_ready, h + 1))
                        if e.new(k_ready, h + 1):
                            pe.wait_ge(k_ready, e.at(k_ready, h + 1))
                        dst = take(s)
                        w = (qi + 1) * P
                        nc.tensor.matmul(dst[:, 0:w], mla_q[0:96, h % 2, qi * P:w], mla_kv[0:96, h % 2, 0:w],
                                         start=True, stop=False)
                        done(nc.tensor.matmul(dst[:, qi * P:w], ident_bf[:], neg_bf[:], start=False, stop=True), s)
                    elif kind == "mla_t":
                        h, qi = s[1:]
                        pe.wait_ge(free[bank_of(("mla_s", h, qi))], e.use(free, ("mla_s", h, qi)))
                        dst = take(s)
                        for k in range(qi + 1):
                            last = nc.tensor.transpose(dst[:, k * P:(k + 1) * P], mla_p[:, qi % 2, k * P:(k + 1) * P], ident)
                        done(last, s)
                    elif kind == "mla_pv":
                        h = s[1]
                        pe.wait_ge(free[bank_of(("mla_t", h, 0))], e.use(free, ("mla_t", h, 0)))
                        pe.wait_ge(free[bank_of(("mla_t", h, 1))], e.use(free, ("mla_t", h, 1)))
                        pe.wait_ge(free[bank_of(("mla_v", h))], e.use(free, ("mla_v", h)))
                        a = 0 if h % 2 == 0 else MLA_DV
                        weighted_values(s, lambda k: v_ones[:, k, a:a + P], mla_pt)
                    elif kind == "ret_s":
                        h, k = s[1:]
                        if e.new(ret_qk_ready, 4):
                            pe.wait_ge(ret_qk_ready, e.at(ret_qk_ready, 4))
                        r = slice(RET_DK * (h % 2), RET_DK * (h % 2) + RET_DK)
                        dst = take(s)
                        done(nc.tensor.matmul(dst[:, 0:SEQ - k * P], ret_k[r, h // 2, k * P:(k + 1) * P],
                                              ret_q[r, h // 2, k * P:], start=True, stop=True), s)
                    elif kind == "ret_pv":
                        h = s[1]
                        pe.wait_ge(free[bank_of(("ret_s", h, 2))], e.use(free, ("ret_s", h, 2)))
                        pe.wait_ge(free[bank_of(("ret_s", h, 3))], e.use(free, ("ret_s", h, 3)))
                        pe.wait_ge(free[bank_of(("ret_v", h))], e.use(free, ("ret_v", h)))
                        weighted_values(s, lambda k: ret_v[:, h, k, :], ret_sc)
                    elif kind == "mod_sum":
                        pe.wait_ge(mod_done, e.at(mod_done, (s[1] + 1) * DT))
                        dst = take(s)
                        for j in range(MOD_W // P):
                            last = nc.tensor.matmul(dst[:, j:j + 1], mod_acc[:, j * P:(j + 1) * P], ones[:, 0:1],
                                                    start=True, stop=True)
                        done(last, s)
            pe.wait_ge(sq_sum_ready, DEPTH + 1)
            nc.tensor.matmul(bank["misc"][:], ones, sq_sum[:], start=True, stop=True).then_inc(fin_sum, 1)

        @block.scalar
        def _(act):
            A = nc.scalar.activation
            act.dma_start(nxt[:], params_nxt[DEPTH]).then_inc(par_in, 16)
            act.dma_start(pos_i[:], positions[0:1, :].to_broadcast([P, SEQ])).then_inc(pos_in, 16)
            for n in range(2 * DT):
                if n >= PRO_RING:
                    act.wait_ge(pro_mod_done, n - PRO_RING + 1)
                act.dma_start(pro_w[:, n % PRO_RING, :], w_mod_first[n]).then_inc(pro_in[n % PRO_RING], 16)
                if n == PRO_RING - 1:
                    act.wait_ge(const_in, 16)
                    A(cond_t[:], c("c"), ACT.Exp, scale=-1.0).then_inc(cond_e, 1)
                if n >= PRO_RING and n - PRO_RING < DT:
                    j = n - PRO_RING
                    act.wait_ge(x_in, 16 * (DT // 2))
                    if j >= 2:
                        act.wait_ge(pro_sum, j - 1)
                    A((sq_t, o_sq)[j % 2][:], x[:, j, :], ACT.Square).then_inc(pro_sq, 1)
            for n, dst in enumerate((sin_mla, cos_mla, sin_ret, cos_ret)):
                act.wait_ge(angles, n + 1)
                A(dst[:], red[:, n, :], ACT.Sin).then_inc(tables, 1)
            act.preload_act_table_set(TABLE_SET)
            with act.Fori(0, DEPTH) as layer:
                e = Counter(act, layer, per_layer)
                gated = []

                def split(i):
                    if i >= N_ITEMS:
                        return
                    n = elements_of(ITEMS[i])
                    act.wait_ge(raw_in[i % RING], e.at(raw_in[i % RING], 16 * (i // RING + 1)))
                    if i >= RING:
                        before = (ITEMS[i - RING], len(tiles_of(ITEMS[i - RING])) - 1)
                        act.wait_ge(full[bank_of(before)], e.use(full, before))
                    A(w_hi[:, i % RING, 0:n], raw[:, i % RING, 0:n], ACT.Copy).then_inc(w_hi_ready, 1)

                def rsqrt_of(key, width):
                    act.wait_ge(full[bank_of(key)], e.use(full, key))
                    src = bank[bank_of(key)]
                    A(rstd[:], src[:], ACT.Ln, scale=1.0 / width, bias=eps).then_inc(free[bank_of(key)], 1)
                    act.wait_ge(free[bank_of(key)], e.use(free, key))
                    A(rstd[:], rstd[:], ACT.Exp, scale=-0.5).then_inc(rstd_ready, 1)

                def gate(it):
                    n = len(gated)
                    if n >= 2 and gated[n - 2][0] not in MERGES:
                        silus = sum(g[0] not in MERGES for g in gated[:n - 1])
                        act.wait_ge(silu_done, e.at(silu_done, silus))
                    elif n >= 2:
                        act.wait_ge(sigma_ready, e.at(sigma_ready, sum(g[0] in MERGES for g in gated[:n - 1])))
                    gated.append(it)
                    x_n, t_n = gate_x[:, n % 2, :], gate_t[:, n % 2, :]
                    act.wait_ge(free[bank_of((it, 0))], e.use(free, (it, 0)))
                    A(t_n, x_n, ACT.Exp, scale=-1.0).then_inc(act_link, 1)
                    act.wait_ge(act_link, e.made(act_link))
                    A(t_n, t_n, ACT.Ln, bias=one).then_inc(act_link, 1)
                    act.wait_ge(act_link, e.made(act_link))
                    if it[0] in MERGES:
                        mixer, j = "abc".index(it[0][1]), it[1]
                        if j >= 3:
                            before = (("p" + it[0][1], (j - 3) // 2), (j - 3) % 2)
                            act.wait_ge(free[bank_of(before)], e.use(free, before))
                        elif mixer:
                            before = (("p" + "abc"[mixer - 1], DT // 2 - 1), 1)
                            act.wait_ge(free[bank_of(before)], e.use(free, before))
                        A(sigma[:, j % 3, :], t_n, ACT.Exp, scale=-1.0).then_inc(sigma_ready, 1)
                    else:
                        A(t_n, t_n, ACT.Exp, scale=-1.0).then_inc(gate_sig, 1)

                def copy_out(key, dst, src=None):
                    act.wait_ge(full[bank_of(key)], e.use(full, key))
                    src = bank[bank_of(key)] if src is None else src
                    A(dst, src[:], ACT.Copy).then_inc(free[bank_of(key)], 1)

                def item(it):
                    i = ITEM_AT[it]
                    kind, j = it
                    if kind in ("q", "g", "bg", "cg", "ma", "mb", "mc"):
                        gate(it)
                        return
                    if kind == "f":
                        act.wait_ge(free[bank_of((it, 0))], e.use(free, (it, 0)))
                        A(hz_b[:], hz_a[:], ACT.Exp, scale=-1.0).then_inc(act_link, 1)
                        act.wait_ge(act_link, e.made(act_link))
                        A(hz_b[:], hz_b[:], ACT.Ln, bias=one).then_inc(hz_ln, 1)
                        act.wait_ge(hz_ln, e.made(hz_ln))
                        A(hz_c[:], hz_b[:], ACT.Exp, scale=-1.0).then_inc(act_link, 1)
                        return
                    if kind == "i":
                        copy_out((it, 0), hg_vt[:])
                    elif kind in ("cq", "ckv"):
                        n = j if kind == "cq" else CQT + j
                        act.wait_ge(full[bank_of((it, 0))], e.use(full, (it, 0)))
                        src = bank[bank_of((it, 0))]
                        if n >= 1:
                            act.wait_ge(cq_sum, e.at(cq_sum, n))
                        A(sq_t[:], src[:], ACT.Square).then_inc(cq_sq, 1)
                        copy_out((it, 0), cq_raw[:, j, :] if kind == "cq" else ckv_raw[:, j, :], src)
                    elif kind == "kr":
                        act.wait_ge(full[bank_of((it, 0))], e.use(full, (it, 0)))
                        src = bank[bank_of((it, 0))]
                        copy_out((it, 0), k_rope[:], src)
                    elif kind == "mla":
                        act.wait_ge(full[bank_of((it, 0))], e.use(full, (it, 0)))
                        src = bank[bank_of((it, 0))]
                        if j >= 2:
                            act.wait_ge(full[bank_of(("mla_s", j - 2, 0))], e.use(full, ("mla_s", j - 2, 0)))
                            act.wait_ge(full[bank_of(("mla_s", j - 2, 1))], e.use(full, ("mla_s", j - 2, 1)))
                        A(mla_q[:, j % 2, :], src[:], ACT.Copy, scale=MLA_SCALE).then_inc(free[bank_of((it, 0))], 1)
                        copy_out((it, 1), mla_kv[:, j % 2, :])
                    elif kind in ("rq", "rk"):
                        act.wait_ge(full[bank_of((it, 0))], e.use(full, (it, 0)))
                        src = bank[bank_of((it, 0))]
                        if kind == "rq" and j == 0:
                            act.dma_start(ret_decay[:], decay).then_inc(decay_in, 16)
                        copy_out((it, 0), (ret_q if kind == "rq" else ret_k)[:, j, :], src)
                    elif kind == "rv":
                        if j >= 2:
                            act.wait_ge(full[bank_of(("ret_v", j - 2))], e.use(full, ("ret_v", j - 2)))
                        copy_out((it, 0), ret_vt[j % 2][:])
                    elif kind == "pc":
                        for m in (2 * j, 2 * j + 1):
                            act.wait_ge(mg_t, e.at(mg_t, m + 1))
                            A(mg_hi[:, m, :], merged[:, m, :], ACT.Copy).then_inc(mg_hi_ready, 1)
                    elif kind == "wo":
                        act.wait_ge(free[bank_of((it, 0))], e.use(free, (it, 0)))
                        if j >= 1:
                            act.wait_ge(x_sum, e.at(x_sum, j))
                        A(sq_t[:], x[:, j, :], ACT.Square).then_inc(x_sq, 1)

                split(0)
                split(1)
                for s in MIXERS_FIRST:
                    kind = s[0]
                    if kind == "norm":
                        rsqrt_of(("ssq",), D_MODEL)
                        act.dma_start(cur[:], params_cur[layer]).then_inc(params_in, 16)
                        act.dma_start(nxt[:], params_nxt[layer]).then_inc(params_in, 16)
                        act.dma_start(mod_w[:, 0, :], w_mod[layer, 0]).then_inc(mod_in[0], 16)
                        for j in range(DT):
                            act.wait_ge(norm_t, e.at(norm_t, j + 1))
                            A(h_hi[:, j, :], (t1, t2)[j % 2][:], ACT.Identity, bias=shift[:, j:j + 1]).then_inc(norm_hi, 1)
                        act.wait_ge(lb_d_ready, e.at(lb_d_ready, 1))
                        A(lb_e[:], lb_e[:], ACT.Exp).then_inc(lb_e_ready, 1)
                    elif kind == "item":
                        item(s[1:])
                    elif kind == "split":
                        split(s[1])
                    elif kind == "hz" and s[2] == 1:
                        act.wait_ge(hz_u, e.at(hz_u, s[1] + 1))
                        act.wait_ge(act_link, e.made(act_link))
                        A(hz_b[:], hz_a[:], ACT.Exp, scale=-1.0).then_inc(hz_s, 1)
                    elif kind == "hz" and s[2] == 2:
                        act.wait_ge(hz_f, e.at(hz_f, s[1] + 1))
                        A(hz_a[:], hz_a[:], ACT.Ln).then_inc(hz_l, 1)
                    elif kind == "hg_v":
                        if s[1] >= 2:
                            act.wait_ge(full[bank_of(("hg_pv", s[1] - 2))], e.use(full, ("hg_pv", s[1] - 2)))
                        copy_out(s, hg_v[:, s[1] % 2, :, :].rearrange("p a b -> p (a b)"))
                    elif kind == "hg_lv":
                        h, n = s[1:]
                        if n <= 6:
                            act.wait_ge(d_ready, e.at(d_ready, 7 * h + n + 1))
                        if n < 5:
                            A(hg_e[:, n % 2, :], hg_e[:, n % 2, :], ACT.Exp).then_inc(e_ready, 1)
                        elif n == 5:
                            act.wait_ge(x_built, e.at(x_built, 7 * h + 5))
                            A(hg_e[:, 0, :], hg_e[:, 1, :], ACT.Exp, scale=-1.0).then_inc(act_link, 1)
                            act.wait_ge(act_link, e.made(act_link))
                            A(hg_e[:, 1, :], hg_e[:, 1, :], ACT.Exp).then_inc(e_ready, 1)
                        elif n == 6:
                            b = hg_b[:, h % 2, :]
                            A(hg_e[:, 0, 0:3 * P], hg_e[:, 0, 0:3 * P], ACT.Exp)
                            A(g_last[:], b.rearrange("p (c t) -> p c t", t=P)[:, :, P - 1], ACT.Exp)
                            A(hg_e[:, 1, 0:3 * P], b[:, P:], ACT.Exp).then_inc(e_ready, 1)
                    elif kind == "hg_cross":
                        h = s[1]
                        if h >= 2:
                            act.wait_ge(full[bank_of(("hg_pv", h - 2))], e.use(full, ("hg_pv", h - 2)))
                        act.wait_ge(full[bank_of(("cross0", h))], e.use(full, ("cross0", h)))
                        src = bank[bank_of(("cross0", h))]
                        A(hg_at[h % 2][:, 0, P:], src[:, 0:3 * P], ACT.Copy)
                        copy_out(("cross0", h), hg_at[h % 2][:, 2, 3 * P:], src[:, 3 * P:])
                        act.wait_ge(full[bank_of(("cross1", h))], e.use(full, ("cross1", h)))
                        src = bank[bank_of(("cross1", h))]
                        copy_out(("cross1", h), hg_at[h % 2][:, 1, 2 * P:], src[:, 0:2 * P])
                    elif kind in ("hg_pv", "ret_pv"):
                        act.wait_ge(full[bank_of(s)], e.use(full, s))
                        src = bank[bank_of(s)]
                        A(o_sq[:], src[:], ACT.Square).then_inc(o_sq_ready, 1)
                    elif kind in ("hg_out", "ret_out"):
                        rsqrt_of(s, HG_DK if kind == "hg_out" else RET_DV)
                        n = s[1] + (0 if kind == "hg_out" else 2 * CH)
                        act.wait_ge(y_t_ready, e.at(y_t_ready, n + 1))
                        A((y_hi if kind == "hg_out" else yc_hi)[:, s[1], :], y_t[:], ACT.Copy).then_inc(y_hi_ready, 1)
                    elif kind in NORM_TILES:
                        if kind != "cq_rest":
                            rsqrt_of(s, D_CQ if kind == "cq_norm" else D_C)
                        raws, his, n0 = (ckv_raw, ckv_hi, CQT) if kind == "ckv_norm" else (cq_raw, cq_hi, 0)
                        for j in NORM_TILES[kind]:
                            act.wait_ge(cqn_t, e.at(cqn_t, n0 + j + 1))
                            A(his[:, j, :], raws[:, j, :], ACT.Copy).then_inc(cqn_hi, 1)
                    elif kind == "ret_v":
                        copy_out(s, ret_v[:, s[1], :, :].rearrange("p a b -> p (a b)"))
                    elif kind == "mla_qk":
                        h = s[1]
                        act.wait_ge(full[bank_of(("mla_v", h))], e.use(full, ("mla_v", h)))
                        src = bank[bank_of(("mla_v", h))]
                        if h >= 2:
                            act.wait_ge(full[bank_of(("mla_pv", h - 2))], e.use(full, ("mla_pv", h - 2)))
                        a = 0 if h % 2 == 0 else 2 * MLA_DV
                        copy_out(("mla_v", h), v_ones[:, :, a:a + MLA_DV],
                                 src[:].rearrange("p (a b) -> p a b", b=P)[:, :, NOPE:])
                    elif kind == "mla_s":
                        h, qi = s[1:]
                        n = CH * h + CH - 1 - qi
                        if n >= 2:
                            before = ("mla_t", (n - 2) // CH, CH - 1 - (n - 2) % CH)
                            act.wait_ge(full[bank_of(before)], e.use(full, before))
                        act.wait_ge(p_max, e.at(p_max, n + 1))
                        src = bank[USES[s][0]]
                        w = (qi + 1) * P
                        A(mla_p[:, qi % 2, 0:w], src[:, 0:w], ACT.Exp, bias=neg_max[:, qi:qi + 1]).then_inc(free[bank_of(s)], 1)
                    elif kind == "mla_t" and s[2] % 2 == 0:
                        h, qi = s[1:]
                        act.wait_ge(full[bank_of(s)], e.use(full, s))
                        src = bank[bank_of(s)]
                        if h >= 1:
                            act.wait_ge(full[bank_of(("mla_pv", h - 1))], e.use(full, ("mla_pv", h - 1)))
                        copy_out(s, mla_pt[:, 0:qi + 1, qi * P:(qi + 1) * P],
                                 src[:, 0:(qi + 1) * P].rearrange("p (a b) -> p a b", b=P))
                    elif kind == "mla_pv":
                        h = s[1]
                        own, other = (slice(0, MLA_DV), slice(MLA_DV, P))[::1 if h % 2 == 0 else -1]
                        act.wait_ge(full[bank_of(s)], e.use(full, s))
                        src = bank[bank_of(s)]
                        A(rstd[own, :], src[other, :], ACT.Ln).then_inc(act_link, 1)
                        act.wait_ge(act_link, e.made(act_link))
                        A(rstd[own, :], rstd[own, :], ACT.Exp, scale=-1.0).then_inc(rstd_ready, 1)
                        if h % 2 == 1:
                            pair = h // 2
                            if pair == 0:
                                act.wait_ge(full[bank_of((("pa", DT // 2 - 1), 1))], e.use(full, (("pa", DT // 2 - 1), 1)))
                            act.wait_ge(y_t_ready, e.at(y_t_ready, CH + pair + 1))
                            A(y_hi[:, pair, :], y_t[:], ACT.Copy).then_inc(y_hi_ready, 1)
                    elif kind == "mod_acc":
                        n = DT * s[1] + s[2] + 1
                        if n < MOD_SECTIONS * DT:
                            if n >= 2:
                                act.wait_ge(mod_done, e.at(mod_done, n - 1))
                            act.dma_start(mod_w[:, n % 2, :], w_mod[layer, n]).then_inc(mod_in[n % 2], 16)
            assert e.own[id(act_link)] == PER_LAYER["act_link"]
            act.wait_ge(fin_sum, 1)
            A(rstd[:], bank["misc"][:], ACT.Ln, scale=1.0 / D_MODEL, bias=eps).then_inc(fin_link, 1)
            act.wait_ge(fin_link, 1)
            A(rstd[:], rstd[:], ACT.Exp, scale=-0.5).then_inc(fin_rstd, 1)

        @block.vector
        def _(dve):
            V = nc.vector
            links = [0]

            def link(ins):
                links[0] += 1
                ins.then_inc(pro_link, 1)
                dve.wait_ge(pro_link, links[0])

            link(V.memset(v_ones[:], 1.0))
            dve.wait_ge(const_in, 16)
            link(V.tensor_copy(ident_bf[:], ident))
            link(V.tensor_copy(neg_bf[:], c("neg")))
            dve.wait_ge(cond_e, 1)
            link(V.tensor_scalar(cond_t[:], cond_t[:], 1.0, None, ALU.add))
            link(V.reciprocal(cond_t[:], cond_t[:]))
            link(V.tensor_tensor(cond[:], cond_t[:], c("c"), ALU.mult))
            def angles_modulo_turn():
                dve.wait_ge(pos_in, 16)
                yield link(V.tensor_copy(pos_f[:], pos_i[:]))
                n = 0
                for inv in ("inv_mla", "inv_ret"):
                    yield link(V.tensor_scalar(ang[:], pos_f[:], c(inv), None, ALU.mult))
                    for quarter in (0.0, 0.25):
                        yield link(V.tensor_scalar(turn[:], ang[:], 1.0 / (2.0 * np.pi), quarter, ALU.mult, ALU.add))
                        yield link(V.tensor_scalar(turn[:], turn[:], ROUND, -ROUND, ALU.add, ALU.add))
                        r = red[:, n, :]
                        yield link(V.scalar_tensor_tensor(r, turn[:], -TWO_PI[0], ang[:], ALU.mult, ALU.add))
                        yield link(V.scalar_tensor_tensor(r, turn[:], -TWO_PI[1], r, ALU.mult, ALU.add))
                        yield link(V.scalar_tensor_tensor(r, turn[:], -TWO_PI[2], r, ALU.mult, ALU.add))
                        yield link(V.tensor_scalar(r, r, quarter * 2.0 * np.pi, PI_BELOW, ALU.add, ALU.min))
                        V.tensor_scalar(r, r, -PI_BELOW, None, ALU.max).then_inc(angles, 1)
                        n += 1

            between = angles_modulo_turn()
            for n in range(2 * DT):
                sec, k = divmod(n, DT)
                acc = pro_acc[:, sec * D_MODEL:(sec + 1) * D_MODEL]
                dve.wait_ge(pro_in[n % PRO_RING], 16 * (n // PRO_RING + 1))
                if k == 0:
                    ins = V.tensor_scalar(acc, pro_w[:, n % PRO_RING, :], cond[:, k:k + 1], None, ALU.mult)
                else:
                    ins = V.scalar_tensor_tensor(acc, pro_w[:, n % PRO_RING, :], cond[:, k:k + 1], acc, ALU.mult, ALU.add)
                ins.then_inc(pro_mod_done, 1)
                dve.wait_ge(pro_mod_done, n + 1)
                next(between, None)
            for _ in between:
                pass
            dve.wait_ge(pro_sum, DT)
            dve.wait_ge(par_in, 16)
            dve.wait_ge(pro_mod_sum, 1)
            link(V.tensor_tensor(shift[:], bank["misc"][:, 0:DT], pn("b_shift"), ALU.add))
            link(V.tensor_tensor(scale_g[:], bank["misc"][:, DT:2 * DT], pn("b_scale"), ALU.add))
            V.scalar_tensor_tensor(scale_g[:], scale_g[:], 1.0, pn("norm_g"), ALU.add, ALU.mult).then_inc(sq_sum_ready, 1)

            with dve.Fori(0, DEPTH) as layer:
                e = Counter(dve, layer, per_layer)
                dve.wait_ge(sq_sum_ready, layer + 1)
                gated = []

                def lo_part(dst, full_value, hi, sig):
                    V.tensor_tensor(dst, full_value, hi.bitcast(F32), ALU.subtract).then_inc(sig, 1)

                def rope(key, src, cos, sin, dst, sig):
                    r, swapped = src
                    dve.wait_ge(full[bank_of(key)], e.use(full, key))
                    ps = bank[bank_of(key)]
                    V.tensor_tensor(t1[swapped, :], r, cos[swapped, :], ALU.mult).then_inc(dve_link, 1)
                    dve.wait_ge(dve_link, e.made(dve_link))
                    V.tensor_tensor(t2[swapped, :], ps[swapped, :], sin[swapped, :], ALU.mult).then_inc(free[bank_of(key)], 1)
                    dve.wait_ge(free[bank_of(key)], e.use(free, key))
                    V.tensor_tensor(dst, t1[swapped, :], t2[swapped, :], ALU.add).then_inc(sig, 1)
                    dve.wait_ge(sig, e.made(sig))

                def mla_rope(t, dst, sig):
                    r, swapped = slice(NOPE, NOPE + ROPE), slice(NOPE + ROPE, P)
                    V.tensor_tensor(t1[r, :], t[r, :], cos_mla[r, :], ALU.mult).then_inc(dve_link, 1)
                    dve.wait_ge(dve_link, e.made(dve_link))
                    V.tensor_tensor(t2[r, :], t[swapped, :], sin_mla[swapped, :], ALU.mult).then_inc(dve_link, 1)
                    dve.wait_ge(dve_link, e.made(dve_link))
                    V.tensor_tensor(dst, t1[r, :], t2[r, :], ALU.add).then_inc(sig, 1)
                    dve.wait_ge(sig, e.made(sig))

                waiting = []

                def bounded(it):
                    n = len(gated)
                    if n >= 2:
                        if gated[n - 2][0] in MERGES:
                            dve.wait_ge(sigma_ready, e.at(sigma_ready, sum(g[0] in MERGES for g in gated[:n - 1])))
                        else:
                            dve.wait_ge(gate_sig, e.at(gate_sig, sum(g[0] not in MERGES for g in gated[:n - 1])))
                    gated.append(it)
                    dve.wait_ge(full[bank_of((it, 0))], e.use(full, (it, 0)))
                    V.tensor_scalar(gate_x[:, n % 2, :], bank[bank_of((it, 0))][:], SIG_MIN, None, ALU.max)\
                        .then_inc(free[bank_of((it, 0))], 1)
                    dve.wait_ge(free[bank_of((it, 0))], e.use(free, (it, 0)))
                    return n

                def silu(it, dst, factor=1.0):
                    waiting.append((bounded(it), dst, factor))

                def finish_silu():
                    while waiting:
                        n, dst, factor = waiting.pop(0)
                        dve.wait_ge(gate_sig, e.at(gate_sig, sum(g[0] not in MERGES for g in gated[:n + 1])))
                        V.scalar_tensor_tensor(dst, gate_x[:, n % 2, :], factor, gate_t[:, n % 2, :], ALU.mult, ALU.mult)\
                            .then_inc(silu_done, 1)
                        dve.wait_ge(silu_done, e.made(silu_done))

                def item(it):
                    kind, j = it
                    if kind == "f":
                        dve.wait_ge(full[bank_of((it, 0))], e.use(full, (it, 0)))
                        V.tensor_scalar(hz_a[:], bank[bank_of((it, 0))][:], SIG_MIN, None, ALU.max)\
                            .then_inc(free[bank_of((it, 0))], 1)
                        dve.wait_ge(free[bank_of((it, 0))], e.use(free, (it, 0)))
                    elif kind == "q":
                        silu(it, hg_q[:, j % 2, :], HG_DK ** -0.5)
                    elif kind == "g":
                        silu(it, hg_g[:, j % 2, :])
                    elif kind == "bg":
                        silu(it, mla_g[:, j % 2, :])
                    elif kind == "cg":
                        silu(it, ret_g[:])
                    elif kind in MERGES:
                        bounded(it)
                    elif kind in ("cq", "ckv"):
                        n = j if kind == "cq" else CQT + j
                        dve.wait_ge(cq_sq, e.at(cq_sq, n + 1))
                        total = (sq_sum if kind == "cq" else ckv_sum)[:]
                        if j == 0:
                            V.tensor_copy(total, sq_t[:]).then_inc(cq_sum, 1)
                            dve.wait_ge(cq_sum, e.made(cq_sum))
                        else:
                            V.tensor_tensor(total, total, sq_t[:], ALU.add).then_inc(cq_sum, 1)
                            dve.wait_ge(cq_sum, e.made(cq_sum))
                    elif kind in ("pa", "pb", "pc"):
                        mixer = "abc".index(kind[1])
                        for t in range(2):
                            m = 2 * j + t
                            dve.wait_ge(full[bank_of((it, t))], e.use(full, (it, t)))
                            ps = bank[bank_of((it, t))]
                            dve.wait_ge(sigma_ready, e.at(sigma_ready, mixer * DT + m + 1))
                            dst = merged[:, m, :] if mixer == 0 else t1[:]
                            V.tensor_tensor(dst, ps[:], sigma[:, m % 3, :], ALU.mult).then_inc(free[bank_of((it, t))], 1)
                            dve.wait_ge(free[bank_of((it, t))], e.use(free, (it, t)))
                            if mixer == 1:
                                V.tensor_tensor(merged[:, m, :], merged[:, m, :], t1[:], ALU.add).then_inc(dve_link, 1)
                                dve.wait_ge(dve_link, e.made(dve_link))
                            elif mixer == 2:
                                V.tensor_tensor(merged[:, m, :], merged[:, m, :], t1[:], ALU.add).then_inc(mg_t, 1)
                                dve.wait_ge(mg_t, e.made(mg_t))
                        if mixer == 2:
                            for m in (2 * j, 2 * j + 1):
                                dve.wait_ge(mg_hi_ready, e.at(mg_hi_ready, m + 1))
                                lo_part(mg_lo[:, m, :], merged[:, m, :], mg_hi[:, m, :], mg_ready)
                    elif kind == "wo":
                        dve.wait_ge(full[bank_of((it, 0))], e.use(full, (it, 0)))
                        ps = bank[bank_of((it, 0))]
                        V.scalar_tensor_tensor(x[:, j, :], ps[:], gate[:, j:j + 1], x[:, j, :], ALU.mult, ALU.add).then_inc(free[bank_of((it, 0))], 1)
                        dve.wait_ge(free[bank_of((it, 0))], e.use(free, (it, 0)))
                        if j >= 1:
                            add_square(j - 1)

                def hz(h, n):
                    if n == 1:
                        dve.wait_ge(hz_ln, e.at(hz_ln, h + 1))
                        V.tensor_tensor(hz_a[:], hz_a[:], hz_b[:], ALU.add).then_inc(hz_u, 1)
                        dve.wait_ge(hz_u, e.made(hz_u))
                    elif n == 2:
                        dve.wait_ge(hz_s, e.at(hz_s, h + 1))
                        V.tensor_scalar(hz_a[:], hz_c[:], one_lb[:, h:h + 1], lb[:, h:h + 1], ALU.mult, ALU.add).then_inc(hz_f, 1)
                        dve.wait_ge(hz_f, e.made(hz_f))
                        V.tensor_scalar(hg_k[:, h % 2, :], hz_b[:], one_lb[:, h:h + 1], None, ALU.mult).then_inc(dve_link, 1)
                        dve.wait_ge(dve_link, e.made(dve_link))
                    else:
                        dve.wait_ge(hz_l, e.at(hz_l, h + 1))
                        V.tensor_tensor_scan(hg_b[:, h % 2, :], c("reset"), hz_a[:], 0.0, ALU.mult, ALU.add).then_inc(b_ready, 1)
                        dve.wait_ge(b_ready, e.made(b_ready))

                def add_square(j):
                    dve.wait_ge(x_sq, e.at(x_sq, j + 1))
                    ins = V.tensor_copy(sq_sum[:], sq_t[:]) if j == 0 else V.tensor_tensor(sq_sum[:], sq_sum[:], sq_t[:], ALU.add)
                    if j < DT - 1:
                        ins.then_inc(x_sum, 1)
                        dve.wait_ge(x_sum, e.made(x_sum))
                    else:
                        ins.then_inc(sq_sum_ready, 1)

                def level_exponents(h, n):
                    b = hg_b[:, h % 2, :]
                    before = 7 * h + (6 if n == 6 else max(n - 1, 0))
                    if before:
                        dve.wait_ge(x_built, e.at(x_built, before))
                    if n < 5:
                        half = LEVELS[n]
                        bv = b.rearrange("p (c s m) -> p c s m", s=2, m=half)
                        ev = hg_e[:, n % 2, :].rearrange("p (c s m) -> p c s m", s=2, m=half)
                        nb = SEQ // (2 * half)
                        ref = bv[:, :, 0, half - 1:half].to_broadcast([P, nb, half])
                        V.tensor_tensor(ev[:, :, 0, :], ref, bv[:, :, 0, :], ALU.subtract)
                        V.tensor_tensor(ev[:, :, 1, :], bv[:, :, 1, :], ref, ALU.subtract).then_inc(d_ready, 1)
                    elif n == 5:
                        bv = b.rearrange("p (c m) -> p c m", m=BASE)
                        V.tensor_tensor(centre[:], bv[:, :, 1], bv[:, :, 2], ALU.add).then_inc(dve_link, 1)
                        dve.wait_ge(dve_link, e.made(dve_link))
                        V.scalar_tensor_tensor(hg_e[:, 1, :].rearrange("p (c m) -> p c m", m=BASE),
                                               centre[:, :, None].to_broadcast([P, SEQ // BASE, BASE]), -0.5, bv,
                                               ALU.mult, ALU.add).then_inc(d_ready, 1)
                    else:
                        bv = b.rearrange("p (c m) -> p c m", m=P)[:, 0:3, :]
                        V.tensor_tensor(hg_e[:, 0, 0:3 * P].rearrange("p (c m) -> p c m", m=P),
                                        bv[:, :, P - 1:P].to_broadcast([P, 3, P]), bv, ALU.subtract).then_inc(d_ready, 1)

                def level_operands(h, n):
                    q, k = hg_q[:, h % 2, :], hg_k[:, h % 2, :]
                    dve.wait_ge(e_ready, e.at(e_ready, 7 * h + n + 1))
                    if 2 <= n < 5:
                        dve.wait_ge(full[bank_of(("lv", h, n - 2))], e.use(full, ("lv", h, n - 2)))
                    elif n == 5:
                        dve.wait_ge(full[bank_of(("lv", h, 3))], e.use(full, ("lv", h, 3)))
                        dve.wait_ge(full[bank_of(("lv", h, 4))], e.use(full, ("lv", h, 4)))
                    elif n < 2 and h:
                        dve.wait_ge(full[bank_of(("lv", h - 1, 5))], e.use(full, ("lv", h - 1, 5)))
                    elif n == 6 and h:
                        dve.wait_ge(full[bank_of(("cross0", h - 1))], e.use(full, ("cross0", h - 1)))
                        dve.wait_ge(full[bank_of(("cross1", h - 1))], e.use(full, ("cross1", h - 1)))
                    if n < 5:
                        def v(t):
                            return t.rearrange("p (c s m) -> p c s m", s=2, m=LEVELS[n])
                        V.tensor_tensor(v(hg_x[:, n % 2, :])[:, :, 0, :], v(hg_e[:, n % 2, :])[:, :, 0, :],
                                        v(k)[:, :, 0, :], ALU.mult)
                        V.tensor_tensor(v(hg_x[:, n % 2, :])[:, :, 1, :], v(hg_e[:, n % 2, :])[:, :, 1, :],
                                        v(q)[:, :, 1, :], ALU.mult).then_inc(x_built, 1)
                    elif n == 5:
                        V.tensor_tensor(hg_x[:, 0, :], hg_e[:, 0, :], k, ALU.mult)
                        V.tensor_tensor(hg_x[:, 1, :], hg_e[:, 1, :], q, ALU.mult).then_inc(x_built, 1)
                    else:
                        def v(t):
                            return t.rearrange("p (c m) -> p c m", m=P)
                        V.tensor_tensor(hg_qc[:, :, 0:P], v(q[:, P:]), v(hg_e[:, 1, 0:3 * P]), ALU.mult).then_inc(dve_link, 1)
                        dve.wait_ge(dve_link, e.made(dve_link))
                        V.tensor_scalar(hg_qc[:, 1, P:2 * P], hg_qc[:, 2, 0:P], g_last[:, 2:3], None, ALU.mult).then_inc(dve_link, 1)
                        dve.wait_ge(dve_link, e.made(dve_link))
                        V.tensor_scalar(hg_qc[:, 0, P:3 * P], hg_qc[:, 1, 0:2 * P], g_last[:, 1:2], None, ALU.mult).then_inc(dve_link, 1)
                        dve.wait_ge(dve_link, e.made(dve_link))
                        V.tensor_tensor(hg_kd[:], hg_e[:, 0, 0:3 * P], k[:, 0:3 * P], ALU.mult).then_inc(x_built, 1)

                def level_select(h, n):
                    dve.wait_ge(full[bank_of(("lv", h, n))], e.use(full, ("lv", h, n)))
                    ps = bank[bank_of(("lv", h, n))]
                    src = ps[:].rearrange("p (c t) -> p c t", t=P)
                    mask = c(("m64", "m32", "m16", "m8", "m4", "mbase")[n])
                    if n == 0:
                        if h >= 2:
                            dve.wait_ge(full[bank_of(("hg_pv", h - 2))], e.use(full, ("hg_pv", h - 2)))
                        ins = V.tensor_tensor(diagonal(hg_at[h % 2]), src, mask[:, None, :].to_broadcast([P, CH, P]), ALU.mult)
                    else:
                        dve.wait_ge(free[bank_of(("lv", h, n - 1))], e.use(free, ("lv", h, n - 1)))
                        V.tensor_copy(carry[:], one)
                        ins = V.copy_predicated(diagonal(hg_at[h % 2]), mask.bitcast(U32)[:, None, :].to_broadcast([P, CH, P]), src)
                    ins.then_inc(free[bank_of(("lv", h, n))], 1)

                def y_out(n, hi, lo):
                    dve.wait_ge(y_hi_ready, e.at(y_hi_ready, n + 1))
                    lo_part(lo, y_t[:], hi, y_ready)

                rstd_uses = [0]

                def next_rstd():
                    rstd_uses[0] += 1
                    dve.wait_ge(rstd_ready, e.at(rstd_ready, rstd_uses[0]))

                for s in MIXERS_FIRST:
                    kind = s[0]
                    if kind == "norm":
                        next_rstd()
                        for j in range(DT + 1):
                            if j < DT:
                                if j >= 2:
                                    dve.wait_ge(h_ready, e.at(h_ready, j - 1))
                                V.scalar_tensor_tensor((t1, t2)[j % 2][:], x[:, j, :], scale_g[:, j:j + 1], rstd[:],
                                                       ALU.mult, ALU.mult).then_inc(norm_t, 1)
                            if j >= 1:
                                i = j - 1
                                dve.wait_ge(norm_hi, e.at(norm_hi, i + 1))
                                V.scalar_tensor_tensor(h_lo[:, i, :], (t1, t2)[i % 2][:], shift[:, i:i + 1],
                                                       h_hi[:, i, :].bitcast(F32), ALU.add, ALU.subtract).then_inc(h_ready, 1)
                        dve.wait_ge(params_in, e.at(params_in, 32))
                        lg = pc("logits").rearrange("p (l h) -> p l h", h=HG_HEADS)
                        V.tensor_tensor(lb_t[:], lg[:, 0, :], lg[:, 1, :], ALU.max).then_inc(dve_link, 1)
                        dve.wait_ge(dve_link, e.made(dve_link))
                        for i in range(2, DEPTH):
                            V.tensor_tensor(lb_t[:], lb_t[:], lg[:, i, :], ALU.max).then_inc(dve_link, 1)
                            dve.wait_ge(dve_link, e.made(dve_link))
                        V.tensor_tensor(lb_e[:], lg, lb_t[:, None, :].to_broadcast([P, DEPTH, HG_HEADS]), ALU.subtract).then_inc(lb_d_ready, 1)
                        dve.wait_ge(lb_d_ready, e.made(lb_d_ready))
                        dve.wait_ge(lb_e_ready, e.at(lb_e_ready, 1))
                        V.tensor_tensor(lb_t[:], lb_e[:, 0, :], lb_e[:, 1, :], ALU.add).then_inc(dve_link, 1)
                        dve.wait_ge(dve_link, e.made(dve_link))
                        for i in range(2, DEPTH):
                            V.tensor_tensor(lb_t[:], lb_t[:], lb_e[:, i, :], ALU.add).then_inc(dve_link, 1)
                            dve.wait_ge(dve_link, e.made(dve_link))
                        V.reciprocal(lb_t[:], lb_t[:]).then_inc(dve_link, 1)
                        dve.wait_ge(dve_link, e.made(dve_link))
                        V.tensor_scalar(lb[:], lb_e[:, 0, :], pc("sel")[:, 0:1], None, ALU.mult).then_inc(dve_link, 1)
                        dve.wait_ge(dve_link, e.made(dve_link))
                        for i in range(1, DEPTH):
                            V.scalar_tensor_tensor(lb[:], lb_e[:, i, :], pc("sel")[:, i:i + 1], lb[:], ALU.mult, ALU.add).then_inc(dve_link, 1)
                            dve.wait_ge(dve_link, e.made(dve_link))
                        V.tensor_tensor(lb[:], lb[:], lb_t[:], ALU.mult).then_inc(dve_link, 1)
                        dve.wait_ge(dve_link, e.made(dve_link))
                        V.tensor_scalar(one_lb[:], lb[:], -1.0, 1.0, ALU.mult, ALU.add).then_inc(dve_link, 1)
                        dve.wait_ge(dve_link, e.made(dve_link))
                    elif kind == "item":
                        finish_silu()
                        item(s[1:])
                    elif kind == "hz":
                        hz(*s[1:])
                    elif kind == "hg_lv":
                        h, n = s[1:]
                        if n < 6:
                            level_exponents(h, n)
                        if n == 1:
                            finish_silu()
                        if n >= 1:
                            level_operands(h, n - 1)
                        if n == 6:
                            level_exponents(h, n)
                        if n >= 2:
                            level_select(h, n - 2)
                    elif kind in ("hg_out", "ret_out"):
                        next_rstd()
                        h = s[1]
                        key = (kind.replace("out", "pv"), h)
                        ps = bank["o"]
                        if kind == "hg_out":
                            ins = V.scalar_tensor_tensor(y_t[:], ps[:], pc("onorm"), rstd[:], ALU.mult, ALU.mult)
                        else:
                            ins = V.tensor_tensor(y_t[:], ps[:], rstd[:], ALU.mult)
                        ins.then_inc(free[bank_of(key)], 1)
                        dve.wait_ge(free[bank_of(key)], e.use(free, key))
                        V.tensor_tensor(y_t[:], y_t[:], hg_g[:, h % 2, :] if kind == "hg_out" else ret_g[:], ALU.mult).then_inc(y_t_ready, 1)
                        dve.wait_ge(y_t_ready, e.made(y_t_ready))
                        if kind == "hg_out":
                            y_out(h, y_hi[:, h, :], y_lo[:, h, :])
                        else:
                            y_out(2 * CH + h, yc_hi[:, h, :], yc_lo[:, h, :])
                    elif kind in NORM_TILES:
                        if kind != "cq_rest":
                            next_rstd()
                        g, raws, his, los, n0 = ((pc("g_cq"), cq_raw, cq_hi, cq_lo, 0) if kind != "ckv_norm" else
                                                    (pc("g_ckv"), ckv_raw, ckv_hi, ckv_lo, CQT))
                        tiles = NORM_TILES[kind]
                        for j in range(tiles.start, tiles.stop + 1):
                            if j < tiles.stop:
                                V.scalar_tensor_tensor(raws[:, j, :], raws[:, j, :], g[:, j:j + 1], rstd[:],
                                                       ALU.mult, ALU.mult).then_inc(cqn_t, 1)
                                dve.wait_ge(cqn_t, e.made(cqn_t))
                            if j > tiles.start:
                                dve.wait_ge(cqn_hi, e.at(cqn_hi, n0 + j))
                                lo_part(los[:, j - 1, :], raws[:, j - 1, :], his[:, j - 1, :], cqn_ready)
                    elif kind == "kr_rope":
                        dve.wait_ge(free[bank_of((("kr", 0), 0))], e.use(free, (("kr", 0), 0)))
                        mla_rope(k_rope, k_rope[NOPE:NOPE + ROPE, :], dve_link)
                    elif kind == "ret_rope":
                        t = (ret_q if s[1] == "rq" else ret_k)[:, s[2], :]
                        rope(s, (t, slice(0, P)), cos_ret, sin_ret, t, ret_qk_ready)
                    elif kind == "mla_qk":
                        h = s[1]
                        r = slice(NOPE, NOPE + ROPE)
                        dve.wait_ge(free[bank_of((("mla", h), 0))], e.use(free, (("mla", h), 0)))
                        mla_rope(mla_q[:, h % 2, :], mla_q[r, h % 2, :], q_ready)
                        dve.wait_ge(full[bank_of(("mla_v", h))], e.use(full, ("mla_v", h)))
                        V.tensor_copy(mla_kv[r, h % 2, :], k_rope[r, :]).then_inc(k_ready, 1)
                        dve.wait_ge(k_ready, e.made(k_ready))
                    elif kind == "mla_s":
                        h, qi = s[1:]
                        dve.wait_ge(full[bank_of(s)], e.use(full, s))
                        ps = bank[bank_of(s)]
                        V.reduce_max(neg_max[:, qi:qi + 1], ps[:, 0:(qi + 1) * P], axis=AX.X, negate=True).then_inc(p_max, 1)
                        dve.wait_ge(p_max, e.made(p_max))
                    elif kind == "mla_t" and s[2] % 2 == 1:
                        h, qi = s[1:]
                        dve.wait_ge(full[bank_of(s)], e.use(full, s))
                        ps = bank[bank_of(s)]
                        if h >= 1:
                            dve.wait_ge(full[bank_of(("mla_pv", h - 1))], e.use(full, ("mla_pv", h - 1)))
                        V.tensor_copy(mla_pt[:, 0:qi + 1, qi * P:(qi + 1) * P],
                                      ps[:, 0:(qi + 1) * P].rearrange("p (a b) -> p a b", b=P)).then_inc(free[bank_of(s)], 1)
                        dve.wait_ge(free[bank_of(s)], e.use(free, s))
                    elif kind == "mla_pv":
                        h = s[1]
                        own = slice(0, MLA_DV) if h % 2 == 0 else slice(MLA_DV, P)
                        next_rstd()
                        V.tensor_tensor(y_t[own, :], bank["o"][own, :], rstd[own, :], ALU.mult).then_inc(free[bank_of(s)], 1)
                        dve.wait_ge(free[bank_of(s)], e.use(free, s))
                        if h % 2 == 1:
                            V.tensor_tensor(y_t[:], y_t[:], mla_g[:, (h // 2) % 2, :], ALU.mult).then_inc(y_t_ready, 1)
                            dve.wait_ge(y_t_ready, e.made(y_t_ready))
                            y_out(CH + h // 2, y_hi[:, h // 2, :], y_lo[:, h // 2, :])
                    elif kind == "ret_s":
                        h, k = s[1:]
                        dve.wait_ge(full[bank_of(s)], e.use(full, s))
                        ps = bank[bank_of(s)]
                        if e.new(decay_in, 16):
                            dve.wait_ge(decay_in, e.at(decay_in, 16))
                        if h >= 1:
                            dve.wait_ge(full[bank_of(("ret_pv", h - 1))], e.use(full, ("ret_pv", h - 1)))
                        V.tensor_tensor(ret_sc[:, k, k * P:], ps[:, 0:SEQ - k * P], ret_decay[:, h, 0:SEQ - k * P],
                                        ALU.mult).then_inc(free[bank_of(s)], 1)
                        dve.wait_ge(free[bank_of(s)], e.use(free, s))
                    elif kind == "mod_acc":
                        sec, k = s[1:]
                        n = DT * sec + k
                        dve.wait_ge(mod_in[n % 2], e.at(mod_in[n % 2], 16 * (n // 2 + 1)))
                        if k == 0:
                            if sec:
                                dve.wait_ge(full[bank_of(("mod_sum", sec - 1))], e.use(full, ("mod_sum", sec - 1)))
                            ins = V.tensor_scalar(mod_acc[:], mod_w[:, n % 2, :], cond[:, k:k + 1], None, ALU.mult)
                        else:
                            ins = V.scalar_tensor_tensor(mod_acc[:], mod_w[:, n % 2, :], cond[:, k:k + 1], mod_acc[:],
                                                         ALU.mult, ALU.add)
                        ins.then_inc(mod_done, 1)
                        dve.wait_ge(mod_done, e.made(mod_done))
                    elif kind == "mod_sum":
                        what, part = divmod(s[1], MOD_SECTIONS // 3)
                        r = slice(part * (MOD_W // P), (part + 1) * (MOD_W // P))
                        dve.wait_ge(full[bank_of(s)], e.use(full, s))
                        ps = bank[bank_of(s)][:, 0:MOD_W // P]
                        dst, bias = ((gate, pc("b_gate")), (shift, pn("b_shift")), (scale_g, pn("b_scale")))[what]
                        V.tensor_tensor(dst[:, r], ps, bias[:, r], ALU.add).then_inc(free[bank_of(s)], 1)
                        dve.wait_ge(free[bank_of(s)], e.use(free, s))
                        if what == 2:
                            V.scalar_tensor_tensor(dst[:, r], dst[:, r], 1.0, pn("norm_g")[:, r], ALU.add, ALU.mult).then_inc(dve_link, 1)
                            dve.wait_ge(dve_link, e.made(dve_link))
                    elif kind == "end":
                        add_square(DT - 1)
            assert e.own[id(dve_link)] == PER_LAYER["dve_link"]
            dve.wait_ge(fin_rstd, 1)
            for j in range(DT):
                V.scalar_tensor_tensor(o_t[:, j, :], x[:, j, :], c("final_g")[:, j:j + 1], rstd[:], ALU.mult, ALU.mult)\
                    .then_inc(fin_out, 1)


def constants():
    cs = np.zeros((P, N_CST), np.float32)

    def put(name, a):
        cs[:, CST[name][0]:CST[name][1]] = a

    i = np.arange(P)
    put("ident", np.eye(P))
    put("ones", 1.0)
    half = RET_DK // 2
    m = np.zeros((P, P))
    for d in i:
        second = (d // half) % 2
        m[d - half if second else d + half, d] = 1.0 if second else -1.0
    put("perm_ret", m)
    for name, half in zip(("m64", "m32", "m16", "m8", "m4"), LEVELS):
        put(name, (i[:, None] // (2 * half) == i[None, :] // (2 * half)) & (i[:, None] % (2 * half) < half)
            & (i[None, :] % (2 * half) >= half))
    put("mbase", (i[:, None] // BASE == i[None, :] // BASE) & (i[:, None] <= i[None, :]))
    put("reset", np.arange(SEQ) % P != 0)
    put("neg", np.where(i[None, :] > i[:, None], -1e30, 0.0))
    turned = np.where((i >= P - ROPE) & (i < P - ROPE // 2), -1.0, 1.0)
    for name, dim, lane, sign in (("inv_mla", ROPE, i % (ROPE // 2), turned), ("inv_ret", RET_DK, i % (RET_DK // 2), 1.0)):
        put(name, (sign * np.float32(10000.0) ** (-(2 * lane).astype(np.float32) / np.float32(dim)))[:, None])
    put("eps", EPS)
    put("one", 1.0)
    log_gamma = np.log1p(-np.exp2(-5.0 - np.arange(RET_HEADS)))
    rel = np.arange(SEQ)[None, :] - i[:, None]
    decay = np.where(rel >= 0, np.exp(log_gamma[:, None, None] * np.maximum(rel, 0)), 0.0) * RET_DK ** -0.5
    return cs, decay.transpose(1, 0, 2).astype(np.float32)


def columns(v, tiles):
    return np.moveaxis(v.reshape(*v.shape[:-1], tiles, P), -1, -2)


def item_weights(item, l, a):
    kind, j = item
    w_in = a["w_in"][l]

    def cols(w, first, n):
        return w[:, first:first + n].reshape(-1, P, n).transpose(1, 0, 2)

    def swapped(w):
        return np.concatenate([w[:, :, ROPE // 2:], w[:, :, :ROPE // 2]], 2)

    at = {"q": "a_q", "f": "a_f", "i": "a_i", "g": "a_g", "cq": "b_cq", "ckv": "b_ckv", "bg": "b_g", "rq": "c_q", "rk": "c_k",
          "rv": "c_v", "cg": "c_g", "ma": "m_a", "mb": "m_b", "mc": "m_c"}
    if kind in at:
        return cols(w_in, OFF[at[kind]] + P * j, P).reshape(P, -1)
    if kind == "kr":
        rope = cols(w_in, OFF["b_kr"], ROPE)
        return np.concatenate([rope, rope, rope, swapped(rope)], 2).reshape(P, -1)
    if kind == "mla":
        uq = cols(a["mla_w_uq"][l], j * (NOPE + ROPE), NOPE + ROPE)
        uq = np.concatenate([uq, swapped(uq[:, :, NOPE:])], 2).reshape(P, -1)
        return np.concatenate([uq, cols(a["mla_w_ukv"][l], j * P, P).reshape(P, -1)], 1)
    if kind in ("pa", "pb", "pc"):
        return cols(a["w_" + kind][l], 2 * P * j, 2 * P).reshape(P, -1)
    return cols(a["w_out"][l], P * j, P).reshape(P, -1)


def lay_out(a):
    a = {k: np.asarray(v) for k, v in a.items()}
    cs, decay = constants()
    cs[:, CST["c"][0]:CST["c"][1]] = columns(a["c"][0], DT)
    cs[:, CST["final_g"][0]:CST["final_g"][1]] = columns(a["final_g"], DT)
    cur = np.zeros((DEPTH, P, N_CUR), np.float32)
    nxt = np.zeros((DEPTH + 1, P, N_NXT), np.float32)
    b = columns(a["b_mod"].reshape(DEPTH, 3, D_MODEL), DT)
    for l in range(DEPTH):
        def put(name, v):
            cur[l][:, CUR[name][0]:CUR[name][1]] = v

        put("b_gate", b[l, 2])
        put("logits", a["hg_lb_logits"].reshape(DEPTH, HG_HEADS, HG_DK).transpose(2, 0, 1).reshape(P, -1))
        put("sel", [float(1 <= j <= l) for j in range(DEPTH)])
        put("onorm", a["hg_onorm_g"][l][:, None])
        put("g_cq", columns(a["mla_g_cq"][l], CQT))
        put("g_ckv", columns(a["mla_g_ckv"][l], CKT))
    for l in range(DEPTH + 1):
        m = (l + 1) % DEPTH if l < DEPTH else 0
        nxt[l] = np.concatenate([columns(a["norm_g"][m], DT), b[m, 0], b[m, 1]], 1)
    w_stream = np.stack([np.concatenate([np.ascontiguousarray(item_weights(it, l, a)).ravel() for it in ITEMS])
                         for l in range(DEPTH)])
    wm = a["w_mod"].reshape(DEPTH, D_MODEL, 3, D_MODEL)
    mixed = np.stack([np.stack([wm[l][:, 2], wm[(l + 1) % DEPTH][:, 0], wm[(l + 1) % DEPTH][:, 1]], 1) for l in range(DEPTH)])
    w_mod = mixed.reshape(DEPTH, DT, P, MOD_SECTIONS, MOD_W).transpose(0, 3, 1, 2, 4).reshape(DEPTH, MOD_SECTIONS * DT, P, MOD_W)
    w_mod_first = wm[0][:, :2].reshape(DT, P, 2, D_MODEL).transpose(2, 0, 1, 3).reshape(2 * DT, P, D_MODEL)
    return {
        "x_t": a["x"][0].T.reshape(DT, P, SEQ).transpose(1, 0, 2),
        "positions": a["positions"],
        "cst": cs, "decay": decay, "params_cur": cur, "params_nxt": nxt,
        "w_stream": w_stream, "w_mod": w_mod, "w_mod_first": w_mod_first,
    }


def kernel(**inputs):
    import concourse.bacc as _bacc
    from concourse.bass_utils import run_bass_kernel_spmd as _run

    arrays = {n: np.ascontiguousarray(v) for n, v in lay_out(inputs).items()}
    nc = _bacc.Bacc("TRN2", target_bir_lowering=False, num_devices=1, dynamic_dma_scratch_size=1024)
    ins = [nc.dram_tensor(n, list(v.shape), mybir.dt.from_np(v.dtype), kind="ExternalInput").ap() for n, v in arrays.items()]
    out = nc.dram_tensor("out_t", [P, DT, SEQ], F32, kind="ExternalOutput").ap()
    build(nc, *ins, out)
    r = _run(nc, [arrays], core_ids=[0])
    out = r.results[0]["out_t"]
    return np.ascontiguousarray(out.transpose(1, 0, 2).reshape(D_MODEL, SEQ).T).reshape(1, SEQ, D_MODEL)
```
